# Optimizing a Trainium2 kernel written in Bass

```python
import jax
import jax.numpy as jnp
from jax import lax
import numpy as np

D_MODEL = 1024
BATCH = 1
SEQ = 512
DEPTH = 2

GRID_W = 64
CTX_LEN = 256
N_MIXERS = 4
N_PER_TYPE = tuple(len(range(m, DEPTH, N_MIXERS)) for m in range(N_MIXERS))
NORM_EPS = 1e-6
CHUNK = 64

HG_DK = 128
HG_HEADS = D_MODEL // HG_DK
HG_DV = D_MODEL // HG_HEADS
HG_WIDTH = HG_HEADS * HG_DK

AT_HD = 64
AT_HEADS = D_MODEL // AT_HD
AT_KV_HEADS = AT_HEADS // 4
AT_GROUP = AT_HEADS // AT_KV_HEADS
AT_Q_DIM = AT_HEADS * AT_HD
AT_KV_DIM = AT_KV_HEADS * AT_HD
AT_QKV_DIM = AT_Q_DIM + 2 * AT_KV_DIM
AT_WINDOW = 128
AT_BLOCK = 128
ROPE_BASE = 10000.0
AXIS_DIM = AT_HD // 2

RT_DK = 256
RT_HEADS = D_MODEL // RT_DK
RT_DV = 2 * RT_DK
RT_QK_DIM = RT_HEADS * RT_DK
RT_V_DIM = RT_HEADS * RT_DV
RT_IN_DIM = 2 * RT_QK_DIM + 2 * RT_V_DIM

RW_HEAD = 64
RW_HEADS = D_MODEL // RW_HEAD
RW_DECAY_LORA = max(32, int(round(1.8 * D_MODEL ** 0.5 / 32)) * 32)
RW_AAA_LORA = max(32, int(round(1.8 * D_MODEL ** 0.5 / 32)) * 32)
RW_GATE_LORA = max(32, int(round(0.6 * D_MODEL ** 0.8 / 32)) * 32)
RW_GN_EPS = 64e-5

D_FF = 2816

kernel_name = 'hybrid_interleaved_dit_trunk'

F32 = jnp.float32

def rms_norm(x, g=None, eps=NORM_EPS):
    xf = x.astype(F32)
    y = xf * lax.rsqrt(jnp.mean(xf * xf, axis=-1, keepdims=True) + eps)
    if g is not None:
        y = y * g.astype(F32)
    return y.astype(x.dtype)

def head_layer_norm(y, w, b, n_heads, eps):
    bsz, s, d = y.shape
    yh = y.reshape(bsz, s, n_heads, d // n_heads).astype(F32)
    mu = jnp.mean(yh, axis=-1, keepdims=True)
    var = jnp.mean(jnp.square(yh - mu), axis=-1, keepdims=True)
    yh = (yh - mu) * lax.rsqrt(var + eps)
    return yh.reshape(bsz, s, d) * w.astype(F32) + b.astype(F32)

def adaln(cvec, w, b):
    m = jax.nn.silu(cvec) @ w + b
    return jnp.split(m[:, None, :], 6, axis=-1)

def modulate(h, shift, scale):
    return h * (1.0 + scale) + shift

def rotate_half(x, n_seg):
    sh = x.shape
    xs = x.reshape(sh[:-1] + (n_seg, 2, sh[-1] // (2 * n_seg)))
    return jnp.concatenate([-xs[..., 1:, :], xs[..., :1, :]], axis=-2).reshape(sh)

def apply_rope(x, cos, sin, n_seg):
    xf = x.astype(F32)
    return (xf * cos + rotate_half(xf, n_seg) * sin).astype(x.dtype)

def axial_rope_tables(n_tokens):
    t = jnp.arange(n_tokens)
    row = (t // GRID_W).astype(F32)
    col = (t % GRID_W).astype(F32)
    inv = ROPE_BASE ** (-jnp.arange(0, AXIS_DIM, 2, dtype=F32) / AXIS_DIM)
    ang_r = row[:, None] * inv[None, :]
    ang_c = col[:, None] * inv[None, :]
    ang = jnp.concatenate([ang_r, ang_r, ang_c, ang_c], axis=-1)
    return jnp.cos(ang), jnp.sin(ang)

def retention_rope_tables(n_tokens):
    t = jnp.arange(n_tokens, dtype=F32)
    inv = ROPE_BASE ** (-jnp.linspace(0.0, 1.0, RT_DK // 2, dtype=F32))
    ang = t[:, None] * inv[None, :]
    ang = jnp.concatenate([ang, ang], axis=-1)
    return jnp.cos(ang), jnp.sin(ang)

def to_chunks(x, n_heads, chunk):
    *lead, b, l, hd = x.shape
    nl = len(lead)
    x = x.reshape(*lead, b, l // chunk, chunk, n_heads, hd // n_heads)
    return x.transpose(*range(nl), nl + 1, nl, nl + 3, nl + 2, nl + 4)

def from_chunks(o):
    n, b, h, c, d = o.shape
    return o.transpose(1, 0, 3, 2, 4).reshape(b, n * c, h * d)

def bidir_chunk_scan(chunk_step, s0, shared, per_dir):
    n = shared[0].shape[0]

    def body(state, j):
        jb = n - 1 - j
        sh = [jnp.stack([a[j], jnp.flip(a[jb], axis=-2)]) for a in shared]
        pd = [jnp.stack([a[0, j], jnp.flip(a[1, jb], axis=-2)]) for a in per_dir]
        return chunk_step(state, *sh, *pd)

    s_final, o = lax.scan(body, s0, jnp.arange(n))
    return o[:, 0] + jnp.flip(o[:, 1], axis=(0, -2)), s_final

def gla_chunk_step(state, q, v, k, g):
    c = q.shape[-2]
    lower = jnp.tril(jnp.ones((c, c), bool))
    b = jnp.cumsum(g, axis=-2)
    o_inter = jnp.einsum('...td,...de->...te', q * jnp.exp(b), state)
    diff = b[..., :, None, :] - b[..., None, :, :]
    decay = jnp.exp(jnp.where(lower[:, :, None], diff, -jnp.inf))
    scores = jnp.einsum('...td,...sd,...tsd->...ts', q, k, decay)
    o_intra = jnp.einsum('...ts,...se->...te', scores, v)
    b_end = b[..., -1:, :]
    state = jnp.exp(b_end[..., 0, :])[..., :, None] * state + jnp.einsum('...sd,...se->...de', k * jnp.exp(b_end - b), v)
    return state, o_inter + o_intra

def make_retention_step(log_gamma):
    lg = log_gamma[..., None]
    idx = jnp.arange(CHUNK, dtype=F32)
    rel = idx[:, None] - idx[None, :]
    intra = jnp.where(rel >= 0, jnp.exp(lg[..., None] * jnp.maximum(rel, 0.0)), 0.0)
    q_in = jnp.exp(lg * (idx + 1.0))[..., None]
    k_out = jnp.exp(lg * (CHUNK - 1.0 - idx))[..., None]
    carry = jnp.exp(lg * CHUNK)[..., None]

    def step(state, q, k, v):
        o = jnp.einsum('...td,...de->...te', q * q_in, state) + jnp.einsum('...ts,...se->...te', jnp.einsum('...td,...sd->...ts', q, k) * intra, v)
        state = carry * state + jnp.einsum('...sd,...se->...de', k * k_out, v)
        return state, o

    return step

def rwkv7_step(state, r, v, kk, w, k, b):
    r, v, kk, w, k, b = (t[..., 0, :] for t in (r, v, kk, w, k, b))
    removed = jnp.einsum('...vk,...k->...v', state, kk)
    state = state * w[..., None, :] - removed[..., :, None] * b[..., None, :] + v[..., :, None] * k[..., None, :]
    y = jnp.einsum('...vk,...k->...v', state, r)
    return state, y[..., None, :]

def qshift_grid(x):
    b, l, d = x.shape
    g = x.reshape(b, l // GRID_W, GRID_W, 4, d // 4)
    p = jnp.pad(g, ((0, 0), (1, 1), (1, 1), (0, 0), (0, 0)))
    return jnp.stack([p[:, 1:-1, :-2, 0], p[:, 1:-1, 2:, 1], p[:, :-2, 1:-1, 2], p[:, 2:, 1:-1, 3]], axis=3).reshape(b, l, d)

def bishift_seq(x):
    h = x.shape[-1] // 2
    prev = jnp.pad(x[:, :-1, :h], ((0, 0), (1, 0), (0, 0)))
    nxt = jnp.pad(x[:, 1:, h:], ((0, 0), (0, 1), (0, 0)))
    return jnp.concatenate([prev, nxt], axis=-1)

def hgrn2_mixer(xc, xl, w_in, lb, norm_g, w_out, need_ctx):
    bsz = xl.shape[0]
    lb = lb.astype(F32)

    def project(x):
        s = x.shape[1]
        q, i_in, gate, zf = jnp.split(x @ w_in, [HG_WIDTH, 2 * HG_WIDTH, 3 * HG_WIDTH], axis=-1)
        zf = zf.reshape(bsz, s, 2, HG_WIDTH).transpose(2, 0, 1, 3).astype(F32)
        log_f = jnp.log(lb + (1.0 - lb) * jax.nn.sigmoid(zf))
        k = (1.0 - lb) * jax.nn.sigmoid(-zf)
        shared = (to_chunks(q.astype(F32), HG_HEADS, CHUNK), to_chunks(i_in.astype(F32), HG_HEADS, CHUNK))
        per_dir = (to_chunks(k, HG_HEADS, CHUNK), to_chunks(log_f, HG_HEADS, CHUNK))
        return shared, per_dir, gate

    def readout(o, gate):
        b_, s, _ = o.shape
        o = rms_norm(o.reshape(b_, s, HG_HEADS, HG_DV), norm_g).reshape(b_, s, HG_WIDTH)
        return (o.astype(xl.dtype) * jax.nn.silu(gate)) @ w_out

    s0 = jnp.zeros((2, bsz, HG_HEADS, HG_DK, HG_DV), F32)
    sh, pd, gate_c = project(xc)
    o_c, s_ctx = bidir_chunk_scan(gla_chunk_step, s0, sh, pd)
    sh, pd, gate_l = project(xl)
    o_l, _ = bidir_chunk_scan(gla_chunk_step, s_ctx, sh, pd)
    out_c = readout(from_chunks(o_c), gate_c) if need_ctx else None
    return out_c, readout(from_chunks(o_l), gate_l)

def sink_attend(q, keys, vals, sink, mask):
    logits = jnp.einsum('bqgrd,bkgd->bgrqk', q, keys).astype(F32) * (AT_HD ** -0.5)
    if mask is not None:
        logits = jnp.where(mask, logits, -jnp.inf)
    s = sink.astype(F32)[None, :, :, None]
    m = jnp.maximum(jnp.max(logits, axis=-1), s)
    p = jnp.exp(logits - m[..., None])
    denom = jnp.sum(p, axis=-1) + jnp.exp(s - m)
    o = jnp.einsum('bgrqk,bkgd->bqgrd', p / denom[..., None], vals.astype(F32))
    return o.astype(q.dtype)

def window_gqa_mixer(xc, xl, w_qkv, b_qkv, sink, w_out, cos, sin, need_ctx):
    bsz, seq, _ = xl.shape
    n_ctx = xc.shape[1]
    sink = sink.reshape(AT_KV_HEADS, AT_GROUP)
    kvc = xc @ w_qkv[:, AT_Q_DIM:] + b_qkv[AT_Q_DIM:]
    kc, vc = [a.reshape(bsz, n_ctx, AT_KV_HEADS, AT_HD) for a in jnp.split(kvc, 2, axis=-1)]
    out_c = None
    if need_ctx:
        qc = (xc @ w_qkv[:, :AT_Q_DIM] + b_qkv[:AT_Q_DIM]).reshape(bsz, n_ctx, AT_KV_HEADS, AT_GROUP, AT_HD)
        out_c = sink_attend(qc, kc, vc, sink, None).reshape(bsz, n_ctx, AT_Q_DIM) @ w_out
    ql, kl, vl = jnp.split(xl @ w_qkv + b_qkv, [AT_Q_DIM, AT_Q_DIM + AT_KV_DIM], axis=-1)
    ql = apply_rope(ql.reshape(bsz, seq, AT_KV_HEADS, AT_GROUP, AT_HD), cos[:, None, None], sin[:, None, None], 2)
    kl = apply_rope(kl.reshape(bsz, seq, AT_KV_HEADS, AT_HD), cos[:, None], sin[:, None], 2)
    vl = vl.reshape(bsz, seq, AT_KV_HEADS, AT_HD)
    pad = ((0, 0), (AT_WINDOW, AT_WINDOW), (0, 0), (0, 0))
    kp, vp = jnp.pad(kl, pad), jnp.pad(vl, pad)
    span = AT_BLOCK + 2 * AT_WINDOW
    n_blk = seq // AT_BLOCK
    ctx_mask = jnp.ones((AT_BLOCK, n_ctx), bool)

    def block(args):
        qb, bi = args
        start = bi * AT_BLOCK
        kw = lax.dynamic_slice_in_dim(kp, start, span, axis=1)
        vw = lax.dynamic_slice_in_dim(vp, start, span, axis=1)
        qpos = start + jnp.arange(AT_BLOCK)
        kpos = start - AT_WINDOW + jnp.arange(span)
        win = (jnp.abs(qpos[:, None] - kpos[None, :]) <= AT_WINDOW) & (kpos >= 0)[None, :] & (kpos < seq)[None, :]
        mask = jnp.concatenate([ctx_mask, win], axis=1)
        return sink_attend(qb, jnp.concatenate([kc, kw], axis=1), jnp.concatenate([vc, vw], axis=1), sink, mask)

    qblocks = ql.reshape(bsz, n_blk, AT_BLOCK, AT_KV_HEADS, AT_GROUP, AT_HD).swapaxes(0, 1)
    ob = lax.map(block, (qblocks, jnp.arange(n_blk)))
    out_l = ob.swapaxes(0, 1).reshape(bsz, seq, AT_Q_DIM) @ w_out
    return out_c, out_l

def retention_mixer(xc, xl, w_in, decay_exp, w_out, cos, sin, need_ctx):
    bsz = xl.shape[0]
    log_gamma = jnp.log1p(-jnp.exp2(decay_exp.astype(F32))).reshape(2, 1, RT_HEADS)
    step = make_retention_step(log_gamma)

    def project(x, rotate):
        s = x.shape[1]
        q, k, v, gate = jnp.split(x @ w_in, [RT_QK_DIM, 2 * RT_QK_DIM, 2 * RT_QK_DIM + RT_V_DIM], axis=-1)
        q = q.reshape(bsz, s, RT_HEADS, RT_DK)
        k = k.reshape(bsz, s, RT_HEADS, RT_DK) * (RT_DK ** -0.5)
        if rotate:
            q = apply_rope(q, cos[:, None], sin[:, None], 1)
            k = apply_rope(k, cos[:, None], sin[:, None], 1)
        shared = (to_chunks(q.reshape(bsz, s, RT_QK_DIM).astype(F32), RT_HEADS, CHUNK),
                  to_chunks(k.reshape(bsz, s, RT_QK_DIM).astype(F32), RT_HEADS, CHUNK),
                  to_chunks(v.astype(F32), RT_HEADS, CHUNK))
        return shared, gate

    def readout(o, gate):
        b_, s, _ = o.shape
        o = rms_norm(o.reshape(b_, s, RT_HEADS, RT_DV)).reshape(b_, s, RT_V_DIM)
        return (jax.nn.silu(gate) * o.astype(xl.dtype)) @ w_out

    s0 = jnp.zeros((2, bsz, RT_HEADS, RT_DK, RT_DV), F32)
    sh, gate_c = project(xc, False)
    o_c, s_ctx = bidir_chunk_scan(step, s0, sh, ())
    sh, gate_l = project(xl, True)
    o_l, _ = bidir_chunk_scan(step, s_ctx, sh, ())
    out_c = readout(from_chunks(o_c), gate_c) if need_ctx else None
    return out_c, readout(from_chunks(o_l), gate_l)

def rwkv7_mixer(xc, xl, mix, w_rkv, w0, w1, w2, a0, a1, a2, g1, g2, k_k, k_a, r_k, ln_w, ln_b, w_out, need_ctx):
    bsz = xl.shape[0]

    def lora(h, wa, wb, act):
        return jnp.einsum('zbsr,zrd->zbsd', act(jnp.einsum('bsd,zdr->zbsr', h, wa)), wb)

    def project(x, shifted):
        s = x.shape[1]
        xx = shifted - x
        r = ((x + xx * mix[0]) @ w_rkv[0]).astype(F32)
        k = ((x + xx * mix[2]) @ w_rkv[1]).astype(F32)
        v = ((x + xx * mix[3]) @ w_rkv[2]).astype(F32)
        w_raw = (w0[:, None, None, :] + lora(x + xx * mix[1], w1, w2, jnp.tanh)).astype(F32)
        decay = jnp.exp(-jnp.exp(-jax.nn.softplus(-w_raw) - 0.5))
        a = jax.nn.sigmoid((a0[:, None, None, :] + lora(x + xx * mix[4], a1, a2, lambda t: t)).astype(F32))
        kkh = (k * k_k.astype(F32)).reshape(bsz, s, RW_HEADS, RW_HEAD)
        kk = (kkh / jnp.maximum(jnp.linalg.norm(kkh, axis=-1, keepdims=True), 1e-12)).reshape(bsz, s, D_MODEL)
        k_dir = k[None] * (1.0 + (a - 1.0) * k_a.astype(F32))
        shared = (to_chunks(r, RW_HEADS, 1), to_chunks(v, RW_HEADS, 1), to_chunks(kk, RW_HEADS, 1))
        per_dir = (to_chunks(decay, RW_HEADS, 1), to_chunks(k_dir, RW_HEADS, 1), to_chunks(kk[None] * a, RW_HEADS, 1))
        return shared, per_dir, (r, k_dir, v, x, xx)

    def readout(y, aux):
        r, k_dir, v, x, xx = aux
        s = y.shape[1]
        rkr = (r * (k_dir[0] + k_dir[1]) * r_k.reshape(-1).astype(F32)).reshape(bsz, s, RW_HEADS, RW_HEAD)
        bonus = (jnp.sum(rkr, axis=-1, keepdims=True) * v.reshape(bsz, s, RW_HEADS, RW_HEAD)).reshape(bsz, s, D_MODEL)
        gate = jax.nn.sigmoid((x + xx * mix[5]) @ g1) @ g2
        y = head_layer_norm(y, ln_w, ln_b, RW_HEADS, RW_GN_EPS) + bonus
        return (y.astype(xl.dtype) * gate) @ w_out

    s0 = jnp.zeros((2, bsz, RW_HEADS, RW_HEAD, RW_HEAD), F32)
    sh, pd, aux_c = project(xc, bishift_seq(xc))
    y_c, s_ctx = bidir_chunk_scan(rwkv7_step, s0, sh, pd)
    sh, pd, aux_l = project(xl, qshift_grid(xl))
    y_l, _ = bidir_chunk_scan(rwkv7_step, s_ctx, sh, pd)
    out_c = readout(from_chunks(y_c), aux_c) if need_ctx else None
    return out_c, readout(from_chunks(y_l), aux_l)

def conv_ffn(h, w_up, conv_w, conv_b, w_down, on_grid):
    bsz, s, _ = h.shape
    u, v = jnp.split(h @ w_up, 2, axis=-1)
    if on_grid:
        u = u.reshape(bsz, s // GRID_W, GRID_W, D_FF)
        rhs = conv_w[:, :, None, :]
    else:
        u = u.reshape(bsz, 1, s, D_FF)
        rhs = conv_w[1:2, :, None, :]
    u = lax.conv_general_dilated(u, rhs.astype(u.dtype), (1, 1), 'SAME', dimension_numbers=('NHWC', 'HWIO', 'NHWC'), feature_group_count=D_FF)
    u = u.reshape(bsz, s, D_FF) + conv_b
    return (jax.nn.gelu(u, approximate=False) * v) @ w_down

def setup_inputs(seed: int = 0) -> dict:
    key = jax.random.key(seed)
    ks = jax.random.split(key, 64)
    counter = iter(range(64))

    def nrm(shape, std):
        return std * jax.random.normal(ks[next(counter)], shape, jnp.float32)

    def unif(shape):
        return jax.random.uniform(ks[next(counter)], shape, jnp.float32)

    d = D_MODEL
    n_a, n_b, n_c, n_d = N_PER_TYPE
    ratio = jnp.arange(d, dtype=jnp.float32) / (d - 1)
    return {
        'x': nrm((BATCH, SEQ, d), 1.0),
        'c': nrm((BATCH, d), 1.0),
        'ctx': nrm((BATCH, CTX_LEN, d), 1.0),
        'c_ctx': nrm((d,), 1.0),
        'ada_w': nrm((DEPTH, d, 6 * d), 0.5 * d ** -0.5),
        'ada_b': nrm((DEPTH, 6 * d), 0.02),
        'norm1_g': 1.0 + nrm((DEPTH, d), 0.1),
        'norm2_g': 1.0 + nrm((DEPTH, d), 0.1),
        'ffn_w_up': nrm((DEPTH, d, 2 * D_FF), d ** -0.5),
        'ffn_conv_w': nrm((DEPTH, 3, 3, D_FF), 1.0 / 3.0),
        'ffn_conv_b': nrm((DEPTH, D_FF), 0.02),
        'ffn_w_down': nrm((DEPTH, D_FF, d), D_FF ** -0.5),
        'hg_w_in': nrm((n_a, d, 5 * HG_WIDTH), d ** -0.5),
        'hg_lb_logits': nrm((DEPTH + 1, HG_WIDTH), 0.5),
        'hg_norm_g': 1.0 + nrm((n_a, HG_DV), 0.1),
        'hg_w_out': nrm((n_a, HG_WIDTH, d), HG_WIDTH ** -0.5),
        'at_w_qkv': nrm((n_b, d, AT_QKV_DIM), d ** -0.5),
        'at_b_qkv': nrm((n_b, AT_QKV_DIM), 0.02),
        'at_sink': nrm((n_b, AT_HEADS), 0.5),
        'at_w_out': nrm((n_b, AT_Q_DIM, d), AT_Q_DIM ** -0.5),
        'rt_w_in': nrm((n_c, d, RT_IN_DIM), d ** -0.5),
        'rt_decay_exp': (-5.0 - jnp.arange(RT_HEADS, dtype=jnp.float32)) + nrm((n_c, 2, RT_HEADS), 0.1),
        'rt_w_out': nrm((n_c, RT_V_DIM, d), RT_V_DIM ** -0.5),
        'rw_mix': unif((n_d, 6, d)),
        'rw_w_rkv': nrm((n_d, 3, d, d), d ** -0.5),
        'rw_w0': (-6.5 + 5.0 * ratio ** 0.85) + nrm((n_d, 2, d), 0.1),
        'rw_w1': nrm((n_d, 2, d, RW_DECAY_LORA), d ** -0.5),
        'rw_w2': nrm((n_d, 2, RW_DECAY_LORA, d), 0.1 * RW_DECAY_LORA ** -0.5),
        'rw_a0': nrm((n_d, 2, d), 0.1),
        'rw_a1': nrm((n_d, 2, d, RW_AAA_LORA), d ** -0.5),
        'rw_a2': nrm((n_d, 2, RW_AAA_LORA, d), 0.5 * RW_AAA_LORA ** -0.5),
        'rw_g1': nrm((n_d, d, RW_GATE_LORA), d ** -0.5),
        'rw_g2': nrm((n_d, RW_GATE_LORA, d), RW_GATE_LORA ** -0.5),
        'rw_k_k': 0.85 + nrm((n_d, d), 0.05),
        'rw_k_a': 1.0 + nrm((n_d, d), 0.05),
        'rw_r_k': -0.04 + nrm((n_d, RW_HEADS, RW_HEAD), 0.02),
        'rw_ln_w': 1.0 + nrm((n_d, d), 0.1),
        'rw_ln_b': nrm((n_d, d), 0.02),
        'rw_w_out': nrm((n_d, d, d), d ** -0.5),
        'final_norm_g': 1.0 + nrm((d,), 0.1),
    }

def reference(x, c, ctx, c_ctx, ada_w, ada_b, norm1_g, norm2_g, ffn_w_up, ffn_conv_w, ffn_conv_b, ffn_w_down,
              hg_w_in, hg_lb_logits, hg_norm_g, hg_w_out, at_w_qkv, at_b_qkv, at_sink, at_w_out,
              rt_w_in, rt_decay_exp, rt_w_out, rw_mix, rw_w_rkv, rw_w0, rw_w1, rw_w2, rw_a0, rw_a1, rw_a2,
              rw_g1, rw_g2, rw_k_k, rw_k_a, rw_r_k, rw_ln_w, rw_ln_b, rw_w_out, final_norm_g):
    seq = x.shape[1]
    cos2, sin2 = axial_rope_tables(seq)
    cos1, sin1 = retention_rope_tables(seq)
    lb_all = jnp.cumsum(jax.nn.softmax(hg_lb_logits.astype(F32), axis=0), axis=0)
    c_ctx_row = c_ctx[None, :]
    xl, xc = x, ctx
    for i in range(DEPTH):
        kind, j = i % N_MIXERS, i // N_MIXERS
        need_ctx = i < DEPTH - 1
        sh1, sc1, g1, sh2, sc2, g2 = adaln(c, ada_w[i], ada_b[i])
        csh1, csc1, cg1, csh2, csc2, cg2 = adaln(c_ctx_row, ada_w[i], ada_b[i])
        hl = modulate(rms_norm(xl, norm1_g[i]), sh1, sc1)
        hc = modulate(rms_norm(xc, norm1_g[i]), csh1, csc1)
        if kind == 0:
            oc, ol = hgrn2_mixer(hc, hl, hg_w_in[j], lb_all[i], hg_norm_g[j], hg_w_out[j], need_ctx)
        elif kind == 1:
            oc, ol = window_gqa_mixer(hc, hl, at_w_qkv[j], at_b_qkv[j], at_sink[j], at_w_out[j], cos2, sin2, need_ctx)
        elif kind == 2:
            oc, ol = retention_mixer(hc, hl, rt_w_in[j], rt_decay_exp[j], rt_w_out[j], cos1, sin1, need_ctx)
        else:
            oc, ol = rwkv7_mixer(hc, hl, rw_mix[j], rw_w_rkv[j], rw_w0[j], rw_w1[j], rw_w2[j], rw_a0[j], rw_a1[j],
                                 rw_a2[j], rw_g1[j], rw_g2[j], rw_k_k[j], rw_k_a[j], rw_r_k[j], rw_ln_w[j],
                                 rw_ln_b[j], rw_w_out[j], need_ctx)
        xl = xl + g1 * ol
        xl = xl + g2 * conv_ffn(modulate(rms_norm(xl, norm2_g[i]), sh2, sc2), ffn_w_up[i], ffn_conv_w[i], ffn_conv_b[i], ffn_w_down[i], True)
        if need_ctx:
            xc = xc + cg1 * oc
            xc = xc + cg2 * conv_ffn(modulate(rms_norm(xc, norm2_g[i]), csh2, csc2), ffn_w_up[i], ffn_conv_w[i], ffn_conv_b[i], ffn_w_down[i], False)
    return rms_norm(xl, final_norm_g)


_drawn_inputs = setup_inputs


def setup_inputs(seed=0):
    import zlib

    import numpy as np

    out = dict(_drawn_inputs(seed))
    spreads = {}
    factors = {'ffn_conv_b': 8.0, 'at_b_qkv': 8.0, 'at_sink': 39.949, 'ctx': 2.706}
    for name, (base, spread) in spreads.items():
        noise = np.random.default_rng([zlib.crc32(name.encode()), seed]).standard_normal(out[name].shape)
        drawn = base * np.exp(spread * noise) if base else spread * noise
        out[name] = jnp.asarray(drawn.astype(out[name].dtype))
    for name, factor in factors.items():
        out[name] = (out[name] * factor).astype(out[name].dtype)
    return out
```

```python
from contextlib import ExitStack

import concourse.bass as bass
from concourse import mybir

F32 = mybir.dt.float32
F32R = mybir.dt.float32r
BF16 = mybir.dt.bfloat16
U8 = mybir.dt.uint8
ALU = mybir.AluOpType
ACT = mybir.ActivationFunctionType
AX = mybir.AxisListType

P = 128
D = 1024
KC = D // P
CTX, LAT = 256, 512
TOK = CTX + LAT
NCH = TOK // P
CCH = CTX // P
FF = 2816
FC = FF // P
GROUPS = (8, 8, 6)
HEADS = 8
GRID_H, GRID_W = LAT // 64, 64
EPS = 1e-6
LEVELS = 7
AT_SCALE = 64 ** -0.5
FWD = list(range(NCH))
BWD = list(range(CCH - 1, -1, -1)) + list(range(NCH - 1, CCH - 1, -1))
assert sum(GROUPS) == FC

PC0, PL0, PE0 = 512 - CTX, 512, 512 + LAT

T_HG, T_HGO = 0, 5 * HEADS
T_FF0 = T_HGO + KC
FF_TILES = 2 * FC + len(GROUPS) * KC
T_AT = T_FF0 + FF_TILES
T_ATO = T_AT + 12
T_FF1 = T_ATO + KC
TILES = T_FF1 + FF_TILES
ADA_GROUPS = 24
ADA_FIRST = 4
SH1, SC1, G1, SH2, SC2, G2 = range(6)

SMALL = {}
_at = 0
for _n, _w in (("c", 2 * KC), ("ada_b", 96), ("n1", 16), ("n2", 16), ("conv", 10 * (2 * FC + 1)),
               ("lb", 24), ("hgn", 1), ("bqkv", 12), ("sink", 16), ("fin", 8)):
    SMALL[_n] = (_at, _at + _w)
    _at += _w
NSMALL = _at


class Tally:

    def __init__(self):
        self.base, self.inner, self.loop = 0, 0, None

    def enter(self, i, per):
        self.base, self.inner, self.loop = self.base + self.inner, 0, (i, per)

    def leave(self, trips):
        assert self.inner == self.loop[1], (self.inner, self.loop[1])
        self.base, self.inner, self.loop = self.base + trips * self.inner, 0, None

    def add(self, n=1):
        self.inner += n
        return self

    def now(self, back=0):
        n = self.base + self.inner - back
        return n if self.loop is None else self.loop[0] * self.loop[1] + n

    def some(self, back=0):
        return self.base + self.inner - back > 0

    def times(self, m, plus):
        n = m * (self.base + self.inner) + plus
        return n if self.loop is None else self.loop[0] * (m * self.loop[1]) + n

    def half(self, back=0, unit=1):
        n = unit * ((self.base + self.inner - back + 1) // 2)
        if self.loop is None:
            return n
        assert self.loop[1] % 2 == 0
        return self.loop[0] * (self.loop[1] // 2 * unit) + n


def trunk(nc, small_in, x_in, ada_in, w_in, ident_in, masks_in, rope_in, rot_in, tri_in, out):
    ctx = ExitStack()
    with ctx:
        def sb(name, shape, dt=F32, scope=ctx):
            return scope.enter_context(nc.sbuf_tensor(name, shape, dt))

        def sem(name):
            return ctx.enter_context(nc.semaphore(name))

        X = sb("X", [P, KC, TOK])
        HH = sb("HH", [P, KC, TOK], F32R)
        HL = sb("HL", [P, KC, TOK], F32R)
        Y = sb("Y", [P, KC, TOK])
        WR = [sb(f"WR{i}", [P, KC, P]) for i in range(2)]
        WH = [sb(f"WH{i}", [P, KC, P], F32R) for i in range(2)]
        WL = [sb(f"WL{i}", [P, KC, P], F32R) for i in range(2)]
        AP_ = [sb(f"ada_piece{i}", [P, 2, 512]) for i in range(2)]
        ident = sb("ident", [P, P])
        ones = sb("ones", [P, 1])
        eps_t = sb("eps_t", [P, 1])
        masks = sb("masks", [P, LEVELS + 1, P], U8)
        small = sb("small", [P, NSMALL])
        silu_c = sb("silu_c", [P, KC, 2])
        sig_c = sb("sig_c", [P, KC, 2])
        ada_row = sb("ada_row", [2, 512])
        ada = sb("ada", [P, 96, 2])
        coef = sb("coef", [P, KC, 2])
        lbt = sb("lbt", [P, 4, HEADS])
        oml = sb("oml", [P, HEADS])
        lbv = sb("lbv", [P, HEADS])
        std6 = sb("std6", [P, NCH])
        rstd6 = sb("rstd6", [P, NCH])
        cw = [sb(f"cw{i}", [P, 10]) for i in range(2)]
        hold = sb("hold", [P, 1])
        hold_act = sb("hold_act", [P, 16])
        hold_pool = sb("hold_pool", [P, 2])

        def part(name):
            a, b = SMALL[name]
            return small[:, a:b]

        c_in = part("c").rearrange("p (k v) -> p k v", v=2)
        ada_b = part("ada_b")
        norm_g = {0: part("n1").rearrange("p (l k) -> p l k", l=2), 1: part("n2").rearrange("p (l k) -> p l k", l=2)}
        conv = part("conv").rearrange("p (n t) -> p n t", t=10)
        hgn = part("hgn")
        bqkv = part("bqkv")
        fin_g = part("fin")

        with ExitStack() as s:
            AD0 = sb("AD0", [P, ADA_FIRST, 4, 1024], F32, s)
        with ExitStack() as s:
            KF = [sb(f"KF{i}", [P, TOK], F32, s) for i in range(2)]
            KB = [sb(f"KB{i}", [P, TOK], F32, s) for i in range(2)]
            CF = [sb(f"CF{i}", [P, TOK], F32, s) for i in range(2)]
            CB = [sb(f"CB{i}", [P, TOK], F32, s) for i in range(2)]
            Q = [sb(f"Q{i}", [P, TOK], F32, s) for i in range(2)]
            VT = sb("VT", [P, TOK], F32, s)
            V = [sb(f"V{i}", [P, TOK], F32, s) for i in range(2)]
            RF = sb("RF", [P, TOK], F32, s)
            RB = sb("RB", [P, TOK], F32, s)
            QL = [sb(f"QL{i}", [P, TOK], F32, s) for i in range(2)]
            KL = [sb(f"KL{i}", [P, TOK], F32, s) for i in range(2)]
            PS = sb("PS", [P, TOK], F32, s)
            SF = sb("SF", [P, NCH - 1, P], F32, s)
            SB = sb("SB", [P, NCH - 1, P], F32, s)
            O1 = sb("O1", [P, TOK], F32, s)
            O2 = sb("O2", [P, TOK], F32, s)
            TF = sb("TF", [P, NCH], F32, s)
            TB = sb("TB", [P, NCH], F32, s)
        with ExitStack() as s:
            GH = sb("GH", [P, max(GROUPS), TOK], F32R, s)
            GL = sb("GL", [P, max(GROUPS), TOK], F32R, s)
            UW = (GRID_H + 2) * (GRID_W + 2)
            UP = [sb(f"UP{i}", [P, UW + CTX + 2], F32, s) for i in range(2)]
            ACC = [sb(f"ACC{i}", [P, TOK], F32, s) for i in range(2)]
        with ExitStack() as s:
            KT = sb("KT", [P, TOK], F32, s)
            AVT = sb("AVT", [P, TOK], F32, s)
            AV = sb("AV", [P, NCH, P], F32, s)
            QT = sb("QT", [P, 4, LAT], F32, s)
            RAW = [sb(f"RAW{i}", [P, LAT], F32, s) for i in range(2)]
            ROT = sb("ROT", [P, LAT], F32, s)
            PB = [sb(f"PB{i}", [P, 5 * P], F32, s) for i in range(3)]
            PT = [sb(f"PT{i}", [P, 5, 4, P], F32, s) for i in range(2)]
            rope = sb("rope", [P, 2, LAT], F32, s)
            rotm = sb("rotm", [P, P], F32, s)
            tri = sb("tri", [P, 3, P], BF16, s)
            nsink = sb("nsink", [P, 16], F32, s)
            mx = [sb(f"mx{i}", [P, 1], F32, s) for i in range(2)]
            nm = [sb(f"nm{i}", [P, 1], F32, s) for i in range(2)]
            den = [sb(f"den{i}", [P, 1], F32, s) for i in range(2)]
            es = [sb(f"es{i}", [P, 1], F32, s) for i in range(2)]
            den2 = [sb(f"den2{i}", [P, 1], F32, s) for i in range(2)]
            rden = [sb(f"rden{i}", [P, 1], F32, s) for i in range(2)]

        SLOT = [ctx.enter_context(nc.psum_tensor(f"slot{i}", [P, 1024], F32)) for i in range(2)]
        MA = ctx.enter_context(nc.psum_tensor("MA", [P, 1024], F32))
        MB = ctx.enter_context(nc.psum_tensor("MB", [P, 1024], F32))

        mask_stage = Y[:, 6:8, :].rearrange("p c t -> p (c t)")[:, 0:(LEVELS + 1) * P]
        SQ = [Y[:, 0, :], Y[:, 1, :]]
        SSQ = Y[:, 2, :]
        NT = [Y[:, 3, :], Y[:, 4, :]]

        small_in_done, x_in_done, const_done, rope_done = sem("small_in_done"), sem("x_in_done"), sem("const_done"), sem("rope_done")
        ada0_in = [sem(f"ada0_in{i}") for i in range(ADA_FIRST)]
        w_in_done = [sem(f"w_in_done{i}") for i in range(2)]
        piece_in = [sem(f"piece_in{i}") for i in range(2)]
        w_hi_done, w_split = sem("w_hi_done"), sem("w_split")
        tile_done = sem("tile_done")
        evacuated = [sem(f"evacuated{i}") for i in range(2)]
        piece_used = sem("piece_used")
        sig_ready, silu_ready, lb_shifted = sem("sig_ready"), sem("silu_ready"), sem("lb_shifted")
        ada_summed, ada_copied, ada_turned, ada_ready = sem("ada_summed"), sem("ada_copied"), sem("ada_turned"), sem("ada_ready")
        sq_ready, sq_added = sem("sq_ready"), sem("sq_added")
        ss_ready, std_ready = sem("ss_ready"), sem("std_ready")
        rstd_ready, rstd_spread = sem("rstd_ready"), sem("rstd_spread")
        normed, hi_ready, lo_ready = sem("normed"), sem("hi_ready"), sem("lo_ready")
        dve_step = sem("dve_step")
        gate_sig = sem("gate_sig")
        level_ready, scores_done, scores_read = sem("level_ready"), sem("scores_done"), sem("scores_read")
        v_turned, v_ready = sem("v_turned"), sem("v_ready")
        kq_final, k_turned, kt_ready = sem("kq_final"), sem("k_turned"), sem("kt_ready")
        kv_done, states_ready = sem("kv_done"), sem("states_ready")
        o_done, o_squared, o_evac, y_ready = sem("o_done"), sem("o_squared"), sem("o_evac"), sem("y_ready")
        conv_done, gelu_done, g_hi, g_lo = sem("conv_done"), sem("gelu_done"), sem("g_hi"), sem("g_lo")
        taps_ready = sem("taps_ready")
        rot_done, roped = sem("rot_done"), sem("roped")
        at_scores, row_max, probs_ready, probs_scaled = sem("at_scores"), sem("row_max"), sem("probs_ready"), sem("probs_scaled")
        p_turned, pt_ready, pv_done, at_out = sem("p_turned"), sem("pt_ready"), sem("pv_done"), sem("at_out")
        out_scaled, out_sent = sem("out_scaled"), sem("out_sent")

        def halves(t, s, which):
            return t[:, :].rearrange("p (n two s) -> p n two s", two=2, s=s)[:, :, which, :]

        def both(t, s, which, at):
            return halves(t, s, which)[:, :, at:at + 1].to_broadcast([P, TOK // (2 * s), s])

        def padded(u):
            return u[:, 0:UW].rearrange("p (h w) -> p h w", w=GRID_W + 2), u[:, UW:]

        def window(bi):
            first = max(bi - 1, 0)
            return first, min(bi + 1, LAT // P - 1) - first + 1

        UNITS = [(bi, half, r) for bi in range(LAT // P) for half in range(2) for r in range(4)]

        def spans(layer_tokens):
            lat = (slice(PL0, PE0), slice(CTX, TOK), 0)
            return [(slice(PC0, PL0), slice(0, CTX), 1), lat] if layer_tokens == TOK else [lat]

        block = ctx.enter_context(nc.Block())

        @block.sync
        def _(sp):
            sp.dma_start(small[:, :], small_in).then_inc(small_in_done, 16)
            for g in range(ADA_FIRST):
                sp.dma_start(AD0[:, g, :, :], ada_in[4 * g:4 * g + 4].rearrange("n p f -> p n f")).then_inc(ada0_in[g], 16)
                if g == 0:
                    sp.dma_start(ident[:, :], ident_in).then_inc(const_done, 16)
                    sp.dma_start(mask_stage, masks_in).then_inc(const_done, 16)
                    sp.dma_start(X[:, :, :], x_in).then_inc(x_in_done, 16)

            split = Tally()

            def load_tile(s, t):
                if split.some(1):
                    sp.wait_ge(w_split, split.now(1))
                split.add()
                sp.dma_start(WR[s][:, :, :], w_in[bass.ds(t, 1)].rearrange("o p k f -> p (o k) f")).then_inc(w_in_done[s], 16)

            used = Tally()

            def load_piece(s, n):
                if used.some(1):
                    sp.wait_ge(piece_used, used.now(1))
                used.add()
                sp.dma_start(AP_[s][:, :, :], ada_in[bass.ds(n, 1)].rearrange("o p (k f) -> p (o k) f", k=2)).then_inc(piece_in[s], 16)

            LEAD = 3
            for t in range(5 + LEAD):
                load_tile(t % 2, t)

            def step_loads(t0, parity, n0, groups):
                left = 4 * groups
                n = 0
                for j in range(5):
                    load_tile((parity + j) % 2, t0 + j)
                    for _ in range(min(left, 3 if j < 4 else left)):
                        load_piece(n % 2, n0 + n)
                        n += 1
                        left -= 1

            n0 = 4 * ADA_FIRST
            step_loads(5 + LEAD, 0, n0, 2)
            with nc.sync.Fori(0, 3) as i:
                split.enter(i, 10)
                used.enter(i, 24)
                step_loads(i * 10 + 10 + LEAD, 1, i * 24 + n0 + 8, 3)
                step_loads(i * 10 + 15 + LEAD, 0, i * 24 + n0 + 20, 3)
                split.leave(3)
                used.leave(3)
            done = 5 + LEAD + 35
            load_tile(done % 2, done)
            done += 1
            half = (T_AT - done) // 2
            assert (T_AT - done) % 2 == 0 and (TILES - T_AT) % 2 == 0 and done % 2 == 0
            with nc.sync.Fori(0, half) as i:
                split.enter(i, 2)
                load_tile(0, i * 2 + done)
                load_tile(1, i * 2 + done + 1)
                split.leave(half)
            for s in range(2):
                sp.wait_ge(evacuated[s], T_AT // 2)
            sp.dma_start(rope[:, :, :], rope_in).then_inc(rope_done, 16)
            sp.dma_start(rotm[:, :], rot_in).then_inc(rope_done, 16)
            sp.dma_start(tri[:, :, :], tri_in).then_inc(rope_done, 16)
            half = (TILES - T_AT) // 2
            with nc.sync.Fori(0, half) as i:
                split.enter(i, 2)
                load_tile(0, i * 2 + T_AT)
                load_tile(1, i * 2 + T_AT + 1)
                split.leave(half)
            for c in range(KC):
                sp.wait_ge(out_scaled, c + 1)
                sp.dma_start(out[:, c, :], Y[:, c, CTX:TOK]).then_inc(out_sent, 16)
            sp.wait_ge(out_sent, 16 * KC)

        @block.gpsimd
        def _(pool):
            n = Tally()

            def split_tile(s, arrived):
                pool.wait_ge(w_in_done[s], arrived)
                if n.some(1):
                    pool.wait_ge(tile_done, n.now(1))
                n.add()
                pool.tensor_tensor(hold_pool[:, s:s + 1], ones[:, :], ones[:, :], ALU.subtract)
                pool.tensor_scalar(WH[s][:, :, :], WR[s][:, :, :], 1.0, 0.0, ALU.mult, ALU.add).then_inc(w_hi_done, 1)
                pool.wait_ge(w_hi_done, n.now())
                pool.tensor_tensor(WL[s][:, :, :], WR[s][:, :, :], WH[s][:, :, :].bitcast(F32), ALU.subtract).then_inc(w_split, 1)

            pool.wait_ge(lb_shifted, 1)
            split_tile(0, 16)
            split_tile(1, 16)
            with nc.gpsimd.Fori(0, TILES // 2 - 1) as i:
                n.enter(i, 2)
                split_tile(0, i * 16 + 32)
                split_tile(1, i * 16 + 32)
                n.leave(TILES // 2 - 1)

        @block.tensor
        def _(pe):
            mm = nc.tensor.matmul
            turn = nc.tensor.transpose
            tile, rows, pieces, stats, sums, parts = Tally(), Tally(), Tally(), Tally(), Tally(), Tally()

            def loop(trips, counts, body):
                with nc.tensor.Fori(0, trips) as i:
                    for t, per in counts:
                        t.enter(i, per)
                    body(i)
                    for t, _ in counts:
                        t.leave(trips)

            def chunk(c):
                return slice(PC0 + c * P, PC0 + (c + 1) * P)

            def begin_tile(s):
                tile.add()
                pe.wait_ge(w_split, tile.now())
                if tile.some(2):
                    pe.wait_ge(evacuated[s], tile.half(2))

            def products(s, half, k, hi, lo, kn=KC):
                po, to, _ = spans(TOK)[half]
                mm(SLOT[s][:, po], WH[s][:, k, :], hi[:, k, to], start=(k == 0), stop=False)
                mm(SLOT[s][:, po], WH[s][:, k, :], lo[:, k, to], start=False, stop=False)
                last = mm(SLOT[s][:, po], WL[s][:, k, :], hi[:, k, to], start=False, stop=(k == kn - 1))
                if half == 1 and k == kn - 1:
                    last.then_inc(tile_done, 1)

            def half_tile(s, half, hi, lo, kn=KC):
                for k in range(kn):
                    products(s, half, k, hi, lo, kn)

            def first_tiles(tokens):
                for s in range(2):
                    begin_tile(s)
                done = parts.now()
                parts.add(KC)
                for k in range(KC):
                    pe.wait_ge(lo_ready, done + k + 1)
                    for s in range(2):
                        for half in range(2) if tokens == TOK else (1,):
                            products(s, half, k, HH, HL)

            def full_tile(s, tokens, hi, lo, kn=KC):
                begin_tile(s)
                if tokens == TOK:
                    half_tile(s, 0, hi, lo, kn)
                half_tile(s, 1, hi, lo, kn)

            def more_tiles(pairs, tokens, hi, lo, kn=KC):
                def body(i):
                    full_tile(0, tokens, hi, lo, kn)
                    full_tile(1, tokens, hi, lo, kn)
                loop(pairs, [(tile, 2)], body)

            def ada_products(piece, k0, first, last):
                for k in range(2):
                    m = mm(MB[0:2, 0:512], silu_c[:, k0 + k, :], piece[:, k, :], start=(first and k == 0), stop=(last and k == 1))
                return m

            def ada_turn():
                pe.wait_ge(ada_copied, rows.now())
                if rows.some(1):
                    pe.wait_ge(ada_ready, rows.now(1))
                for m in range(4):
                    last = mm(MB[:, 512 + 2 * m:514 + 2 * m], ada_row[0:2, m * P:(m + 1) * P], ident[0:2, 0:2], start=True, stop=True)
                last.then_inc(ada_turned, 1)

            def ada_group():
                for k in range(4):
                    pieces.add()
                    pe.wait_ge(piece_in[k % 2], pieces.half(0, 16))
                    last = ada_products(AP_[k % 2], 2 * k, k == 0, k == 3)
                    last.then_inc(piece_used, 1)
                rows.add()

            pe.wait_ge(silu_ready, 1)
            pe.wait_ge(const_done, 32)
            for g in range(ADA_FIRST):
                pe.wait_ge(ada0_in[g], 16)
                for k in range(4):
                    last = ada_products(AD0[:, g, k, :].rearrange("p (k f) -> p k f", k=2), 2 * k, k == 0, k == 3)
                last.then_inc(ada_summed, 1)
                rows.add()
                ada_turn()

            def token_sums(src, first):
                stats.add()
                for c in range(first, NCH):
                    last = mm(MA[:, c:c + 1], src[:, c * P:(c + 1) * P], ones[:, :], start=True, stop=True)
                last.then_inc(ss_ready, 1)

            def spread(first):
                pe.wait_ge(rstd_ready, stats.now())
                for c in range(first, NCH):
                    last = mm(MB[:, chunk(c)], rstd6[:, c:c + 1].to_broadcast([P, P]), ident[:, :], start=True, stop=True)
                last.then_inc(rstd_spread, 1)

            def norm_pe(first):
                sums.add(KC - 1)
                pe.wait_ge(sq_added, sums.now())
                pe.wait_ge(ada_ready, rows.now())
                token_sums(SSQ, first)
                spread(first)

            level, head = Tally(), Tally()

            def level_scores(b, n):
                level.add()
                pe.wait_ge(level_ready, level.now())
                if level.some(1):
                    pe.wait_ge(scores_read, level.now(1))
                q = QL[n % 2] if n < LEVELS else Q[b]
                for c in range(NCH):
                    t = slice(c * P, (c + 1) * P)
                    last = mm(MA[:, chunk(c)], KL[n % 2][:, t], q[:, t], start=True, stop=True)
                last.then_inc(scores_done, 1)

            def value_turn(b):
                for c in range(NCH):
                    last = turn(MB[:, chunk(c)], VT[:, c * P:(c + 1) * P], ident[:, :])
                last.then_inc(v_turned, 1)

            def key_value(b):
                pe.wait_ge(kq_final, head.now())
                pe.wait_ge(scores_read, level.now())
                pe.wait_ge(ada_ready, rows.now())
                pe.wait_ge(v_ready, head.now())
                for src, dst in ((KF, MB), (KB, MA)):
                    for c in range(NCH):
                        last = turn(dst[:, chunk(c)], src[b][:, c * P:(c + 1) * P], ident[:, :])
                    last.then_inc(k_turned, 1)
                for n, (kt, dst, order) in enumerate(((RF, MB, FWD), (RB, MA, BWD))):
                    pe.wait_ge(kt_ready, head.times(2, n - 1))
                    for c in order[:-1]:
                        t = slice(c * P, (c + 1) * P)
                        last = mm(dst[:, chunk(c)], kt[:, t], V[b][:, t], start=True, stop=True)
                    last.then_inc(kv_done, 1)

            def outputs(b):
                pe.wait_ge(states_ready, head.times(2, 0))
                for c in range(NCH):
                    t = slice(c * P, (c + 1) * P)
                    f, k = FWD.index(c), BWD.index(c)
                    last = mm(MB[:, chunk(c)], V[b][:, t], PS[:, t], start=True, stop=(f == 0 and k == 0))
                    if f > 0:
                        last = mm(MB[:, chunk(c)], SF[:, f - 1, :], CF[b][:, t], start=False, stop=(k == 0))
                    if k > 0:
                        last = mm(MB[:, chunk(c)], SB[:, k - 1, :], CB[b][:, t], start=False, stop=True)
                last.then_inc(o_done, 1)

            def head_sums():
                pe.wait_ge(o_squared, head.now())
                token_sums(O2, 0)

            def head_spread():
                pe.wait_ge(o_evac, head.now())
                spread(0)

            def head_step(b, parity, groups, tail=True, project=True):
                def between(n):
                    if tail and n == 0:
                        key_value(1 - b)
                    if tail and n == 1:
                        outputs(1 - b)
                    if tail and n == 2:
                        head_sums()
                    if n == 3:
                        if tail:
                            head_spread()
                        level_scores(b, 0)
                    if n == 4:
                        if tail:
                            pe.wait_ge(y_ready, head.now())
                        head.add()
                        value_turn(b)
                    if n >= 4:
                        level_scores(b, n - 3)
                    if n == 5 and groups:
                        pe.wait_ge(v_ready, head.now())
                    if 5 < n <= 5 + groups:
                        ada_turn()
                    if 5 <= n < 5 + groups:
                        ada_group()
                    if n == 9:
                        level_scores(b, LEVELS)

                for n in range(10):
                    if project:
                        s = (parity + n // 2) % 2
                        if n % 2 == 0:
                            begin_tile(s)
                        half_tile(s, n % 2, HH, HL)
                    between(n)

            norm_pe(0)
            first_tiles(TOK)
            for j in range(2, 5):
                full_tile(j % 2, TOK, HH, HL)
            head_step(0, 1, 2, tail=False)

            def two_heads(i):
                head_step(1, 0, 3)
                head_step(0, 1, 3)
            loop(3, [(tile, 10), (rows, 6), (pieces, 24), (level, 16), (head, 2), (stats, 2)], two_heads)
            for s in range(2):
                pe.wait_ge(evacuated[s], T_HGO // 2)
            head_step(1, 0, 0, project=False)
            key_value(1)
            outputs(1)
            head_sums()
            head_spread()
            first_tiles(TOK)
            more_tiles(KC // 2 - 1, TOK, HH, HL)

            gated = Tally()

            def feed_forward(tokens):
                gated.add(2)
                for g, n in enumerate(GROUPS):
                    if g == 0:
                        first_tiles(tokens)
                    more_tiles(n - (g == 0), tokens, HH, HL)
                    gated.add(n)
                    begin_tile(0)
                    for k in range(n):
                        if k in (0, n - 1):
                            pe.wait_ge(g_lo, gated.now(k == 0))
                        for half in range(2) if tokens == TOK else (1,):
                            products(0, half, k, GH, GL, n)
                    full_tile(1, tokens, GH, GL, n)
                    more_tiles(KC // 2 - 1, tokens, GH, GL, n)

            norm_pe(0)
            feed_forward(TOK)

            norm_pe(0)
            pe.wait_ge(rope_done, 48)
            rot, unit, block_n, vals = Tally(), Tally(), Tally(), Tally()
            vals.base = HEADS
            rot.base = 2

            def rotate(b, s, back=0):
                pe.wait_ge(evacuated[s], tile.half(back))
                rot.add()
                pe.wait_ge(roped, rot.now(1))
                mm(MA[:, 0:LAT], rotm[:, :], RAW[b][:, :], start=True, stop=True).then_inc(rot_done, 1)

            def at_score(u, bi, half, r):
                hp = slice(64 * half, 64 * half + 64)
                S = (MA, MB)[u % 2]
                first, n = window(bi)
                if u >= 2:
                    pe.wait_ge(probs_ready, unit.times(1, (u - 1)))
                q = QT[hp, r, bi * P:(bi + 1) * P]
                mm(S[:, PC0:PL0], q, KT[hp, 0:CTX], start=True, stop=True)
                edges = ([(0, 0)] if bi > 0 else []) + ([(n - 1, 1)] if bi < LAT // P - 1 else [])
                mm(S[:, PL0:PL0 + n * P], q, KT[hp, CTX + first * P:CTX + (first + n) * P], start=True, stop=False)
                for e, (at, which) in enumerate(edges):
                    last = mm(S[:, PL0 + at * P:PL0 + (at + 1) * P], tri[:, 2, :], tri[:, which, :], start=False, stop=(e == len(edges) - 1))
                last.then_inc(at_scores, 1)

            def at_turn(u, bi, half, r):
                pe.wait_ge(probs_scaled, unit.times(1, (u + 1)))
                if u >= 1:
                    pe.wait_ge(pt_ready, unit.times(1, u))
                for c in range(2 + window(bi)[1]):
                    last = turn(SLOT[0][:, chunk(c)], PB[u % 3][:, c * P:(c + 1) * P], ident[:, :])
                last.then_inc(p_turned, 1)

            def at_values(v, bi, half):
                first, n = window(bi)
                pe.wait_ge(pt_ready, unit.times(1, (4 * v + 4)))
                if half == 0 and bi > 0:
                    pe.wait_ge(at_out, block_n.times(1, bi))
                for j, c in enumerate([0, 1] + [CCH + first + j for j in range(n)]):
                    last = mm(SLOT[1][64 * half:64 * half + 64, 0:512], AV[:, c, 64 * half:64 * half + 64],
                              PT[v % 2][:, j, :, :].rearrange("p r q -> p (r q)"), start=(j == 0), stop=(j == n + 1))
                last.then_inc(pv_done, 1)

            def two_key_heads(i):
                first_tiles(TOK)
                parts.inner -= KC
                rotate(0, 0, 1)
                full_tile(0, LAT, HH, HL)
                pe.wait_ge(evacuated[1], tile.half(1))
                for c in range(NCH):
                    last = turn(MB[:, chunk(c)], AVT[:, c * P:(c + 1) * P], ident[:, :])
                last.then_inc(v_turned, 1)
                rotate(1, 0)
                for r in range(1, 4):
                    full_tile(r % 2, LAT, HH, HL)
                    rotate((r + 1) % 2, r % 2)
                vals.add()
                pe.wait_ge(v_ready, vals.now())
                pe.wait_ge(roped, rot.now())
                at_score(0, *UNITS[0])
                at_score(1, *UNITS[1])
                for u in range(len(UNITS)):
                    if u + 2 < len(UNITS):
                        at_score(u + 2, *UNITS[u + 2])
                    if u % 4 == 0 and u:
                        at_values(u // 4 - 1, *UNITS[u - 1][:2])
                    at_turn(u, *UNITS[u])
                at_values(7, *UNITS[-1][:2])
                unit.add(len(UNITS))
                block_n.add(LAT // P)
                pe.wait_ge(at_out, block_n.now())

            loop(2, [(tile, 6), (rot, 5), (unit, 32), (block_n, 4), (vals, 1)], two_key_heads)
            parts.add(KC)
            first_tiles(LAT)
            more_tiles(KC // 2 - 1, LAT, HH, HL)
            norm_pe(CCH)
            feed_forward(LAT)
            norm_pe(CCH)

        @block.scalar
        def _(act):
            go = nc.scalar.activation
            tile, squares, norms, stats = Tally(), Tally(), Tally(), Tally()
            his, added = Tally(), Tally()

            def loop(trips, counts, body):
                with nc.scalar.Fori(0, trips) as i:
                    for t, per in counts:
                        t.enter(i, per)
                    body(i)
                    for t, _ in counts:
                        t.leave(trips)

            def next_tile():
                tile.add()
                act.wait_ge(tile_done, tile.now())

            act.wait_ge(small_in_done, 16)
            go(sig_c[:, :, :], c_in, ACT.Sigmoid).then_inc(sig_ready, 1)
            act.wait_ge(lb_shifted, 1)
            go(lbt[:, 0:3, :], lbt[:, 0:3, :], ACT.Exp).then_inc(sig_ready, 1)

            def carry(n):
                go(hold_act[:, n:n + 1], hold_act[:, n:n + 1], ACT.Copy)

            def token_std(scale, first):
                stats.add()
                act.wait_ge(ss_ready, stats.now())
                go(std6[:, first:NCH], MA[:, first:NCH], ACT.Sqrt, bias=eps_t[:, :], scale=scale).then_inc(std_ready, 1)

            def norm_act(tokens, shift, tiles=None):
                t = slice(TOK - tokens, TOK)
                for c in range(KC):
                    if tiles is not None:
                        act.wait_ge(evacuated[c % 2], tiles // 2 + c // 2 + 1)
                    if c >= 2:
                        act.wait_ge(sq_added, added.now() + max(1, c - 2))
                    go(SQ[c % 2][:, t], X[:, c, t], ACT.Square).then_inc(sq_ready, 1)
                added.add(KC - 1)
                token_std(1.0 / D, (TOK - tokens) // P)
                if shift is None:
                    return
                for c in range(KC):
                    norms.add()
                    act.wait_ge(normed, norms.now())
                    for _, to, v in spans(tokens):
                        last = go(HH[:, c, to], NT[c % 2][:, to], ACT.Identity, bias=ada[:, shift + c, v:v + 1])
                    last.then_inc(hi_ready, 1)

            def mixer_hi(tokens):
                t = slice(TOK - tokens, TOK)
                for c in range(KC):
                    go(HH[:, c, t], Y[:, c, t], ACT.Copy).then_inc(hi_ready, 1)

            head = Tally()

            def decays(c, k, s):
                next_tile()
                go(c[:, :], SLOT[s][:, PC0:PE0], ACT.Sigmoid)
                go(k[:, :], SLOT[s][:, PC0:PE0], ACT.Sigmoid, scale=-1.0).then_inc(evacuated[s], 1)

            def query(b, s, h):
                next_tile()
                carry(b)
                go(Q[b][:, :], SLOT[s][:, PC0:PE0], ACT.Copy, scale=oml[:, bass.ds(h, 1)]).then_inc(evacuated[s], 1)

            def values(s):
                next_tile()
                go(VT[:, :], SLOT[s][:, PC0:PE0], ACT.Copy).then_inc(evacuated[s], 1)

            def gate(s, h):
                next_tile()
                carry(2 + s)
                go(Y[:, bass.ds(h, 1), :].rearrange("p o t -> p (o t)"), SLOT[s][:, PC0:PE0], ACT.Sigmoid).then_inc(gate_sig, 1)

            def value_copy(b):
                act.wait_ge(v_turned, head.now())
                go(V[b][:, :], MB[:, PC0:PE0], ACT.Copy).then_inc(v_ready, 1)

            def key_copies():
                for n, (dst, src) in enumerate(((RF, MB), (RB, MA))):
                    act.wait_ge(k_turned, head.times(2, n - 1))
                    go(dst[:, :], src[:, PC0:PE0], ACT.Copy).then_inc(kt_ready, 1)

            def output_copies():
                act.wait_ge(o_done, head.now())
                go(O2[:, :], MB[:, PC0:PE0], ACT.Square).then_inc(o_squared, 1)
                go(O1[:, :], MB[:, PC0:PE0], ACT.Copy, scale=hgn).then_inc(o_evac, 1)

            def head_step(b, parity, h, tail=True, project=True):
                s = parity
                if tail:
                    key_copies()
                    output_copies()
                if project:
                    decays(CF[1 - b], KF[1 - b], s)
                if tail:
                    token_std(1.0 / P, 0)
                if project:
                    decays(CB[1 - b], KB[1 - b], 1 - s)
                head.add()
                value_copy(b)
                if project:
                    query(1 - b, s, h + 1)
                    values(1 - s)
                    gate(s, h + 1)

            act.wait_ge(x_in_done, 16)
            norm_act(TOK, SH1 * KC)
            decays(CF[0], KF[0], 0)
            decays(CB[0], KB[0], 1)
            query(0, 0, 0)
            values(1)
            gate(0, 0)
            head_step(0, 1, 0, tail=False)

            def two_heads(i):
                head_step(1, 0, i * 2 + 1)
                head_step(0, 1, i * 2 + 2)
            loop(3, [(tile, 10), (head, 2), (stats, 2)], two_heads)
            head_step(1, 0, 7, project=False)
            key_copies()
            output_copies()
            token_std(1.0 / P, 0)
            act.wait_ge(y_ready, HEADS)
            mixer_hi(TOK)
            tile.add(KC)

            def feed_forward(tokens):
                freed.add(2)
                for n in GROUPS:
                    def body(i):
                        for b in range(2):
                            next_tile()
                            act.wait_ge(g_lo, freed.now(1))
                            freed.add()
                            conv_n.add()
                            act.wait_ge(taps_ready, conv_n.now())
                            lat, cx = padded(UP[b])
                            go(lat[:, 1:1 + GRID_H, 1:1 + GRID_W], SLOT[0][:, PL0:PE0].rearrange("p (h w) -> p h w", w=GRID_W), ACT.Copy)
                            if tokens == TOK:
                                go(cx[:, 1:1 + CTX], SLOT[0][:, PC0:PL0], ACT.Copy)
                            t0 = TOK - tokens
                            go(ACC[b][:, t0:TOK], SLOT[0][:, PE0 - tokens:PE0], ACT.Identity, scale=cw[b][:, 4:5], bias=cw[b][:, 9:10]).then_inc(evacuated[0], 1)
                            tile.add()
                            act.wait_ge(conv_done, conv_n.now())
                            go(ACC[b][:, t0:TOK], ACC[b][:, t0:TOK], ACT.Gelu).then_inc(gelu_done, 1)
                            act.wait_ge(evacuated[1], tile.half())
                            carry(4 + b)
                            go(GH[:, bass.ds(i * 2 + b, 1), t0:TOK].rearrange("p o t -> p (o t)"), ACC[b][:, t0:TOK], ACT.Copy).then_inc(g_hi, 1)
                    loop(n // 2, [(tile, 4), (conv_n, 2), (freed, 2)], body)
                    tile.add(KC)

            conv_n, freed = Tally(), Tally()
            norm_act(TOK, SH2 * KC, T_HGO)
            feed_forward(TOK)
            norm_act(TOK, 48 + SH1 * KC, T_AT - KC)

            rot, unit, pair = Tally(), Tally(), Tally()

            def at_exp(u, i, half, r):
                hd = bass.ds(i * 8 + (half * 4 + r), 1)
                S = (MA, MB)[u % 2]
                n = 2 + window(UNITS[u][0])[1]
                act.wait_ge(row_max, unit.times(1, (u + 1)))
                if u >= 3:
                    act.wait_ge(p_turned, unit.times(1, (u - 2)))
                go(PB[u % 3][:, 0:n * P], S[:, PC0:PC0 + n * P], ACT.Exp, scale=AT_SCALE, bias=nm[u % 2][:, :], accum_out=den[u % 2][:, :])
                go(es[u % 2][:, :], nsink[:, hd], ACT.Exp, scale=-1.0, bias=nm[u % 2][:, :]).then_inc(probs_ready, 1)

            def at_copy(u):
                bi, half, r = UNITS[u]
                n = 2 + window(bi)[1]
                v = u // 4
                act.wait_ge(p_turned, unit.times(1, (u + 1)))
                if v >= 2 and r == 0:
                    act.wait_ge(pv_done, pair.times(1, (v - 1)))
                go(PT[v % 2][:, 0:n, r, :], SLOT[0][:, PC0:PC0 + n * P].rearrange("p (n q) -> p n q", q=P), ACT.Copy).then_inc(pt_ready, 1)

            def two_key_heads(i):
                def raw(b, s, j):
                    act.wait_ge(roped, rot.now(1))
                    rot.add()
                    carry(6 + j)
                    go(RAW[b][:, :], SLOT[s][:, PL0:PE0], ACT.Identity, bias=bqkv[:, bass.ds(i * 6 + j, 1)]).then_inc(evacuated[s], 1)
                next_tile()
                carry(12)
                go(KT[:, 0:CTX], SLOT[0][:, PC0:PL0], ACT.Identity, bias=bqkv[:, bass.ds(i * 6, 1)])
                raw(0, 0, 0)
                next_tile()
                carry(13)
                go(AVT[:, :], SLOT[1][:, PC0:PE0], ACT.Identity, bias=bqkv[:, bass.ds(i * 6 + 1, 1)]).then_inc(evacuated[1], 1)
                next_tile()
                raw(1, 0, 2)
                vals.add()
                act.wait_ge(v_turned, vals.now())
                go(AV[:, :, :], MB[:, PC0:PE0].rearrange("p (c f) -> p c f", f=P), ACT.Copy).then_inc(v_ready, 1)
                for r in range(1, 4):
                    next_tile()
                    raw((r + 1) % 2, r % 2, 2 + r)
                at_exp(0, i, *UNITS[0][1:])
                at_exp(1, i, *UNITS[1][1:])
                for u in range(len(UNITS)):
                    at_copy(u)
                    if u + 2 < len(UNITS):
                        at_exp(u + 2, i, *UNITS[u + 2][1:])
                unit.add(len(UNITS))
                pair.add(8)

            vals = Tally()
            vals.base, rot.base = HEADS, 2
            loop(2, [(tile, 6), (rot, 5), (unit, 32), (pair, 8), (vals, 1)], two_key_heads)
            act.wait_ge(at_out, 8)
            mixer_hi(LAT)
            tile.add(KC)
            norm_act(LAT, 48 + SH2 * KC, T_ATO)
            feed_forward(LAT)
            norm_act(LAT, None, TILES - KC)

        @block.vector
        def _(dve):
            tt, ts, stt, cp = nc.vector.tensor_tensor, nc.vector.tensor_scalar, nc.vector.scalar_tensor_tensor, nc.vector.tensor_copy
            tile, steps, rows, stats = Tally(), Tally(), Tally(), Tally()
            squares, added, his, spreads = Tally(), Tally(), Tally(), Tally()

            def loop(trips, counts, body):
                with nc.vector.Fori(0, trips) as i:
                    for t, per in counts:
                        t.enter(i, per)
                    body(i)
                    for t, _ in counts:
                        t.leave(trips)

            def mark(ins):
                steps.add()
                ins.then_inc(dve_step, 1)

            def settle():
                dve.wait_ge(dve_step, steps.now())

            def link(ins):
                mark(ins)
                settle()

            mark(nc.vector.memset(ones[:, :], 1.0))
            mark(nc.vector.memset(eps_t[:, :], EPS))
            mark(nc.vector.memset(hold[:, :], 0.0))
            mark(nc.vector.memset(hold_act[:, :], 0.0))
            dve.wait_ge(small_in_done, 16)
            lb = part("lb").rearrange("p (l h) -> p l h", l=3)
            link(tt(lbt[:, 3, :], lb[:, 0, :], lb[:, 1, :], ALU.max))
            link(tt(lbt[:, 3, :], lbt[:, 3, :], lb[:, 2, :], ALU.max))
            for n in range(3):
                last = tt(lbt[:, n, :], lb[:, n, :], lbt[:, 3, :], ALU.subtract)
            last.then_inc(lb_shifted, 1)
            dve.wait_ge(sig_ready, 1)
            tt(silu_c[:, :, :], c_in, sig_c[:, :, :], ALU.mult).then_inc(silu_ready, 1)
            dve.wait_ge(sig_ready, 2)
            link(tt(lbt[:, 3, :], lbt[:, 0, :], lbt[:, 1, :], ALU.add))
            link(tt(lbt[:, 3, :], lbt[:, 3, :], lbt[:, 2, :], ALU.add))
            link(nc.vector.reciprocal(lbt[:, 3, :], lbt[:, 3, :]))
            link(tt(lbv[:, :], lbt[:, 0, :], lbt[:, 3, :], ALU.mult))
            link(ts(oml[:, :], lbv[:, :], -1.0, 1.0, ALU.mult, ALU.add))

            def ada_copy(first=False):
                rows.add()
                if first:
                    dve.wait_ge(ada_summed, rows.now())
                else:
                    dve.wait_ge(piece_used, rows.times(4, -4 * ADA_FIRST))
                cp(ada_row[0:2, :], MB[0:2, 0:512]).then_inc(ada_copied, 1)

            def ada_add(j):
                dve.wait_ge(ada_turned, rows.now())
                tt(ada[:, bass.ds(j, 4), :], MB[:, 512:520].rearrange("p (m v) -> p m v", v=2),
                   ada_b[:, bass.ds(j, 4)].unsqueeze(2).to_broadcast([P, 4, 2]), ALU.add).then_inc(ada_ready, 1)

            for g in range(ADA_FIRST):
                ada_copy(True)
                ada_add(4 * g)

            def token_rstd(first):
                stats.add()
                dve.wait_ge(std_ready, stats.now())
                nc.vector.reciprocal(rstd6[:, first:NCH], std6[:, first:NCH]).then_inc(rstd_ready, 1)

            def add_square(c, tokens):
                t = slice(TOK - tokens, TOK)
                if c == 0:
                    return
                dve.wait_ge(sq_ready, squares.now() + c + 1)
                if c > 1:
                    dve.wait_ge(sq_added, added.now())
                added.add()
                tt(SSQ[:, t], SQ[0][:, t] if c == 1 else SSQ[:, t], SQ[c % 2][:, t], ALU.add).then_inc(sq_added, 1)

            def norm_dve(tokens, gain, scale, shift):
                t = slice(TOK - tokens, TOK)
                squares.add(KC)
                if scale is not None:
                    dve.wait_ge(ada_ready, rows.now())
                    link(stt(coef[:, :, :], ada[:, scale:scale + KC, :], 1.0, gain.unsqueeze(2).to_broadcast([P, KC, 2]), ALU.add, ALU.mult))
                token_rstd((TOK - tokens) // P)
                dve.wait_ge(rstd_spread, stats.now())
                if scale is None:
                    for c in range(KC):
                        stt(Y[:, c, t], X[:, c, t], gain[:, c:c + 1], MB[:, PL0:PE0], ALU.mult, ALU.mult).then_inc(out_scaled, 1)
                    return

                lows = his.base + his.inner

                def scaled(c):
                    if c >= 2:
                        dve.wait_ge(lo_ready, lows + c - 1)
                    for po, to, v in spans(tokens):
                        last = stt(NT[c % 2][:, to], X[:, c, to], coef[:, c, v:v + 1], MB[:, po], ALU.mult, ALU.mult)
                    last.then_inc(normed, 1)

                def low(c):
                    his.add()
                    dve.wait_ge(hi_ready, his.now())
                    for _, to, v in spans(tokens):
                        last = stt(HL[:, c, to], NT[c % 2][:, to], ada[:, shift + c, v:v + 1], HH[:, c, to].bitcast(F32), ALU.add, ALU.subtract)
                    last.then_inc(lo_ready, 1)
                scaled(0)
                for c in range(KC):
                    if c + 1 < KC:
                        scaled(c + 1)
                    low(c)

            def mixer_lo(tokens):
                t = slice(TOK - tokens, TOK)
                for c in range(KC):
                    his.add()
                    dve.wait_ge(hi_ready, his.now())
                    tt(HL[:, c, t], Y[:, c, t], HH[:, c, t].bitcast(F32), ALU.subtract).then_inc(lo_ready, 1)

            def residual(tokens, gate):
                def body(i):
                    for s in range(2):
                        tile.add()
                        dve.wait_ge(tile_done, tile.now())
                        for po, to, v in spans(tokens):
                            x = X[:, bass.ds(i * 2 + s, 1), to].rearrange("p o t -> p (o t)")
                            g = ada[:, bass.ds(i * 2 + (gate + s), 1), v:v + 1].rearrange("p o v -> p (o v)")
                            last = stt(x, SLOT[s][:, po], g, x, ALU.mult, ALU.add)
                        last.then_inc(evacuated[s], 1)
                loop(KC // 2, [(tile, 2)], body)

            def last_residual(tokens, gate):
                for c in range(KC):
                    tile.add()
                    dve.wait_ge(tile_done, tile.now())
                    for po, to, v in spans(tokens):
                        last = stt(X[:, c, to], SLOT[c % 2][:, po], ada[:, gate + c, v:v + 1], X[:, c, to], ALU.mult, ALU.add)
                    last.then_inc(evacuated[c % 2], 1)
                    if c > 0:
                        add_square(c - 1, tokens)
                add_square(KC - 1, tokens)

            head, level = Tally(), Tally()

            def forget(b, parity, h):
                tile.add(2)
                dve.wait_ge(evacuated[parity], tile.half())
                tile.add()
                dve.wait_ge(evacuated[1 - parity], tile.half())
                tile.add(2)
                for c in (CF, CB):
                    mark(ts(c[b][:, :], c[b][:, :], oml[:, bass.ds(h, 1)], lbv[:, bass.ds(h, 1)], ALU.mult, ALU.add))
                settle()

            def products(b, n):
                s = 2 ** n
                level.add()
                q, k = QL[n % 2], KL[n % 2]
                tt(halves(q, s, 1), halves(Q[b], s, 1), halves(CF[b], s, 1), ALU.mult)
                tt(halves(q, s, 0), halves(Q[b], s, 0), halves(CB[b], s, 0), ALU.mult)
                if n == 0:
                    cp(halves(k, s, 0), halves(KF[b], s, 0))
                    cp(halves(k, s, 1), halves(KB[b], s, 1)).then_inc(level_ready, 1)
                else:
                    tt(halves(k, s, 0), halves(KF[b], s, 0), halves(RF, s, 0), ALU.mult)
                    tt(halves(k, s, 1), halves(KB[b], s, 1), halves(RB, s, 1), ALU.mult).then_inc(level_ready, 1)

            def diagonal(b):
                level.add()
                tt(KL[1][:, :], KF[b][:, :], KB[b][:, :], ALU.add).then_inc(level_ready, 1)

            def double(b, n):
                s = 2 ** n
                dve.wait_ge(level_ready, level.now())
                if n == 0:
                    mark(nc.vector.memset(halves(RF, s, 1), 1.0))
                    mark(nc.vector.memset(halves(RB, s, 0), 1.0))
                    mark(cp(halves(RF, s, 0), halves(CF[b], s, 1)))
                    mark(cp(halves(RB, s, 1), halves(CB[b], s, 0)))
                else:
                    mark(tt(halves(RF, s, 0), halves(RF, s, 0), both(CF[b], s, 1, s - 1), ALU.mult))
                    mark(tt(halves(RB, s, 1), halves(RB, s, 1), both(CB[b], s, 0, 0), ALU.mult))
                settle()
                mark(tt(halves(CF[b], s, 1), halves(CF[b], s, 1), both(CF[b], s, 0, s - 1), ALU.mult))
                mark(tt(halves(CB[b], s, 0), halves(CB[b], s, 0), both(CB[b], s, 1, 0), ALU.mult))
                settle()

            def take(n, back):
                dve.wait_ge(scores_done, level.now(back))
                if level.some(back + 1):
                    dve.wait_ge(scores_read, level.now(back + 1))
                mark(nc.vector.memset(hold[:, :], 0.0))
                for c in range(2):
                    t = slice(c * TOK // 2, (c + 1) * TOK // 2)
                    last = nc.vector.copy_predicated(
                        PS[:, t].rearrange("p (c t) -> p c t", t=P), masks[:, n:n + 1, :].to_broadcast([P, NCH // 2, P]),
                        MA[:, PC0 + t.start:PC0 + t.stop].rearrange("p (c t) -> p c t", t=P))
                last.then_inc(scores_read, 1)

            def finals(b):
                mark(cp(TF[:, :], CF[b][:, :].rearrange("p (c t) -> p c t", t=P)[:, :, P - 1:P].rearrange("p c o -> p (c o)")))
                mark(cp(TB[:, :], CB[b][:, :].rearrange("p (c t) -> p c t", t=P)[:, :, 0:1].rearrange("p c o -> p (c o)")))
                settle()
                mark(tt(CF[b][:, :], CF[b][:, :], Q[b][:, :], ALU.mult))
                mark(tt(CB[b][:, :], CB[b][:, :], Q[b][:, :], ALU.mult))
                tt(KF[b][:, :], KF[b][:, :], RF[:, :], ALU.mult)
                tt(KB[b][:, :], KB[b][:, :], RB[:, :], ALU.mult).then_inc(kq_final, 1)

            def states():
                settle()
                for n, (st, total, src, order) in enumerate(((SF, TF, MB, FWD), (SB, TB, MA, BWD))):
                    dve.wait_ge(kv_done, head.times(2, n - 1))
                    for j, c in enumerate(order[:-1]):
                        kv = src[:, PC0 + c * P:PC0 + (c + 1) * P]
                        if j == 0:
                            ins = cp(st[:, 0, :], kv)
                        else:
                            ins = stt(st[:, j, :], st[:, j - 1, :], total[:, c:c + 1], kv, ALU.mult, ALU.add)
                        if j < NCH - 2:
                            link(ins)
                    ins.then_inc(states_ready, 1)

            def head_out(h):
                dve.wait_ge(rstd_spread, stats.now())
                link(tt(O1[:, :], O1[:, :], MB[:, PC0:PE0], ALU.mult))
                y = Y[:, bass.ds(h, 1), :].rearrange("p o t -> p (o t)")
                tt(y, y, O1[:, :], ALU.mult).then_inc(y_ready, 1)

            def gate(s, h):
                dve.wait_ge(gate_sig, gates.add().now())
                y = Y[:, bass.ds(h, 1), :].rearrange("p o t -> p (o t)")
                tt(y, y, SLOT[s][:, PC0:PE0], ALU.mult).then_inc(evacuated[s], 1)

            gates = Tally()

            def head_step(b, parity, h, j0, groups, tail=True, project=True):
                forget(b, parity, h)
                products(b, 0)
                if tail:
                    states()
                double(b, 0)
                products(b, 1)
                if tail:
                    token_rstd(0)
                    head_out(h - 1)
                head.add()
                take(0, 1)
                for n in range(2, LEVELS):
                    double(b, n - 1)
                    products(b, n)
                    take(n - 1, 1)
                    g = n - 3
                    if 0 <= g - 1 < groups:
                        ada_add(j0 + 4 * (g - 1))
                    if 0 <= g < groups:
                        ada_copy()
                diagonal(b)
                take(LEVELS - 1, 1)
                double(b, LEVELS - 1)
                finals(b)
                take(LEVELS, 0)
                if project:
                    gate(parity, h + 1)

            for c in range(KC):
                add_square(c, TOK)
            norm_dve(TOK, norm_g[0][:, 0, :], SC1 * KC, SH1 * KC)
            dve.wait_ge(const_done, 32)
            mark(cp(masks[:, :, :].rearrange("p n t -> p (n t)"), mask_stage))
            link(nc.vector.memset(PS[:, :], 0.0))
            gate(0, 0)
            j0 = 4 * ADA_FIRST
            head_step(0, 1, 0, j0, 2, tail=False)

            def two_heads(i):
                head_step(1, 0, i * 2 + 1, i * 24 + (j0 + 8), 3)
                head_step(0, 1, i * 2 + 2, i * 24 + (j0 + 20), 3)
            loop(3, [(tile, 10), (rows, 6), (level, 16), (head, 2), (stats, 2), (gates, 2), (steps, 2 * 53)], two_heads)
            head_step(1, 0, 7, 0, 0, project=False)
            states()
            token_rstd(0)
            head_out(7)
            mixer_lo(TOK)
            last_residual(TOK, G1 * KC)
            norm_dve(TOK, norm_g[1][:, 0, :], SC2 * KC, SH2 * KC)

            conv_n = Tally()

            def feed_forward(tokens, layer):
                t0 = TOK - tokens
                for b in range(2):
                    nc.vector.memset(UP[b][:, :], 0.0).then_inc(g_lo, 1)
                n0 = layer * FC
                if layer == 0:
                    cp(cw[0][:, :], conv[:, 0, :]).then_inc(taps_ready, 1)
                for g, n in enumerate(GROUPS):
                    def body(i):
                        for b in range(2):
                            tile.add()
                            dve.wait_ge(evacuated[0], tile.half())
                            conv_n.add()
                            cp(cw[1 - b][:, :], conv[:, bass.ds(i * 2 + (n0 + b + 1), 1), :].rearrange("p o t -> p (o t)")).then_inc(taps_ready, 1)
                            lat, cx = padded(UP[b])
                            acc = ACC[b][:, CTX:TOK].rearrange("p (h w) -> p h w", w=GRID_W)
                            taps = [k for k in range(9) if k != 4]
                            dve.wait_ge(taps_ready, conv_n.now())
                            for j, k in enumerate(taps):
                                if tokens == TOK and j < 2:
                                    o = 2 * j
                                    mark(stt(ACC[b][:, 0:CTX], cx[:, o:o + CTX], cw[b][:, 3 + o:4 + o], ACC[b][:, 0:CTX], ALU.mult, ALU.add))
                                dy, dx = k // 3, k % 3
                                ins = stt(acc, lat[:, dy:dy + GRID_H, dx:dx + GRID_W], cw[b][:, k:k + 1], acc, ALU.mult, ALU.add)
                                if j < len(taps) - 1:
                                    link(ins)
                                else:
                                    ins.then_inc(conv_done, 1)
                            tile.add()
                            dve.wait_ge(gelu_done, conv_n.now())
                            dve.wait_ge(tile_done, tile.now())
                            tt(ACC[b][:, t0:TOK], ACC[b][:, t0:TOK], SLOT[1][:, PE0 - tokens:PE0], ALU.mult).then_inc(evacuated[1], 1)
                            dve.wait_ge(g_hi, conv_n.now())
                            tt(GL[:, bass.ds(i * 2 + b, 1), t0:TOK].rearrange("p o t -> p (o t)"), ACC[b][:, t0:TOK],
                               GH[:, bass.ds(i * 2 + b, 1), t0:TOK].rearrange("p o t -> p (o t)").bitcast(F32), ALU.subtract).then_inc(g_lo, 1)
                    loop(n // 2, [(tile, 4), (conv_n, 2), (steps, 2 * (7 + (2 if tokens == TOK else 0)))], body)
                    n0 += n
                    (residual if g < len(GROUPS) - 1 else last_residual)(tokens, 48 * layer + G2 * KC)

            feed_forward(TOK, 0)
            norm_dve(TOK, norm_g[0][:, 1, :], 48 + SC1 * KC, 48 + SH1 * KC)

            ts(nsink[:, :], part("sink"), -1.0, None, ALU.mult).then_inc(roped, 1)
            nc.vector.memset(hold[:, :], 0.0).then_inc(roped, 1)
            dve.wait_ge(roped, 2)
            dve.wait_ge(rope_done, 48)
            rot, unit, pair, block_n = Tally(), Tally(), Tally(), Tally()

            def rope_one(dst, b):
                rot.add()
                dve.wait_ge(rot_done, rot.now())
                mark(tt(dst, RAW[b][:, :], rope[:, 0, :], ALU.mult))
                mark(tt(ROT[:, :], MA[:, 0:LAT], rope[:, 1, :], ALU.mult))
                settle()
                tt(dst, dst, ROT[:, :], ALU.add).then_inc(roped, 1)

            def at_max(u, i):
                bi, half, r = UNITS[u]
                hd = bass.ds(i * 8 + (half * 4 + r), 1)
                S = (MA, MB)[u % 2]
                n = 2 + window(bi)[1]
                dve.wait_ge(at_scores, unit.times(1, (u + 1)))
                link(nc.vector.tensor_reduce(mx[u % 2][:, :], S[:, PC0:PC0 + n * P], AX.X, ALU.max))
                ts(nm[u % 2][:, :], mx[u % 2][:, :], -AT_SCALE, nsink[:, hd], ALU.mult, ALU.min).then_inc(row_max, 1)

            def at_scale(u):
                n = 2 + window(UNITS[u][0])[1]
                dve.wait_ge(probs_ready, unit.times(1, (u + 1)))
                link(tt(den[u % 2][:, :], den[u % 2][:, :], es[u % 2][:, :], ALU.add))
                link(nc.vector.reciprocal(rden[u % 2][:, :], den[u % 2][:, :]))
                ts(PB[u % 3][:, 0:n * P], PB[u % 3][:, 0:n * P], rden[u % 2][:, :], None, ALU.mult).then_inc(probs_scaled, 1)

            def at_evac(bi, i):
                dve.wait_ge(pv_done, pair.now() + 2 * (bi + 1))
                cp(Y[:, bass.ds(i * 4, 4), CTX + bi * P:CTX + (bi + 1) * P], SLOT[1][:, 0:512].rearrange("p (r q) -> p r q", q=P)).then_inc(at_out, 1)

            def two_key_heads(i):
                rope_one(KT[:, CTX:TOK], 0)
                for r in range(4):
                    rope_one(QT[:, r, :], (r + 1) % 2)
                at_max(0, i)
                at_max(1, i)
                for u in range(len(UNITS)):
                    at_scale(u)
                    if u + 2 < len(UNITS):
                        at_max(u + 2, i)
                    if u % 8 == 0 and u:
                        at_evac(u // 8 - 1, i)
                at_evac(3, i)
                unit.add(32)
                pair.add(8)
                tile.add(6)

            loop(2, [(tile, 6), (rot, 5), (unit, 32), (pair, 8), (steps, 10 + 3 * 32)], two_key_heads)
            mixer_lo(LAT)
            last_residual(LAT, 48 + G1 * KC)
            norm_dve(LAT, norm_g[1][:, 1, :], 48 + SC2 * KC, 48 + SH2 * KC)
            feed_forward(LAT, 1)
            norm_dve(LAT, fin_g, None, None)


def kernel(**inputs):
    import ml_dtypes
    import numpy as np
    import concourse.bacc as bacc
    from concourse.bass_utils import run_bass_kernel_spmd

    a = {k: np.asarray(v) for k, v in inputs.items()}
    f = np.float32

    def cols(v):
        return np.ascontiguousarray(v.reshape(-1, P).T)

    def tiles(w):
        k, n = w.shape
        if k < D:
            w = np.concatenate([w, np.zeros((D - k, n), w.dtype)])
        return w.reshape(KC, P, n // P, P).transpose(2, 1, 0, 3)

    x = np.concatenate([a["ctx"][0], a["x"][0]]).T.reshape(KC, P, TOK).transpose(1, 0, 2)

    wq = a["at_w_qkv"][0]
    nq = 1024
    heads = [(g * 4 + r) for kt in range(2) for r in range(4) for g in (2 * kt, 2 * kt + 1)]
    perm = np.concatenate([np.arange(h * 64, h * 64 + 64) for h in heads])
    at_cols = []
    for kt in range(2):
        at_cols += [np.arange(nq + kt * P, nq + (kt + 1) * P), np.arange(nq + 256 + kt * P, nq + 256 + (kt + 1) * P)]
        at_cols += [perm[(4 * kt + r) * P:(4 * kt + r + 1) * P] for r in range(4)]
    at_cols = np.concatenate(at_cols)

    def feed(layer):
        up, down = a["ffn_w_up"][layer], a["ffn_w_down"][layer]
        u, v = tiles(up[:, :FF]), tiles(up[:, FF:])
        out, at = [], 0
        for n in GROUPS:
            for c in range(at, at + n):
                out += [u[c:c + 1], v[c:c + 1]]
            out.append(tiles(down[at * P:(at + n) * P]))
            at += n
        return out

    hg = tiles(a["hg_w_in"][0]).reshape(5, HEADS, P, KC, P)
    hg = hg[[3, 4, 0, 1, 2]].transpose(1, 0, 2, 3, 4).reshape(5 * HEADS, P, KC, P)
    w = np.concatenate([hg, tiles(a["hg_w_out"][0])] + feed(0) + [tiles(wq[:, at_cols]), tiles(a["at_w_out"][0][perm])] + feed(1))
    assert w.shape[0] == TILES, (w.shape, TILES)

    ada = a["ada_w"].reshape(2, 4, 2, P, 12, 512).transpose(0, 4, 1, 3, 2, 5).reshape(96, P, 1024)

    taps = np.concatenate([a["ffn_conv_w"].reshape(2, 9, FC, P), a["ffn_conv_b"].reshape(2, 1, FC, P)], axis=1)
    taps = taps.transpose(3, 0, 2, 1).reshape(P, 2 * FC * 10)
    cc = np.stack([a["c"][0], a["c_ctx"]], axis=1)
    order = [g * 4 + r for kt in range(2) for g in (2 * kt, 2 * kt + 1) for r in range(4)]
    packed = {
        "c": cc.reshape(KC, P, 2).transpose(1, 0, 2).reshape(P, 2 * KC),
        "ada_b": cols(a["ada_b"].reshape(-1)), "n1": cols(a["norm1_g"].reshape(-1)), "n2": cols(a["norm2_g"].reshape(-1)),
        "conv": np.concatenate([taps, np.zeros((P, 10), f)], axis=1),
        "lb": cols(a["hg_lb_logits"].reshape(-1)), "hgn": cols(a["hg_norm_g"].reshape(-1)),
        "bqkv": cols(a["at_b_qkv"][0][at_cols]), "sink": np.broadcast_to(a["at_sink"][0][order], (P, 16)),
        "fin": cols(a["final_norm_g"]),
    }
    small = np.concatenate([packed[n].astype(f, copy=False) for n in SMALL], axis=1)
    assert small.shape[1] == NSMALL

    i = np.arange(P)
    masks = np.zeros((P, LEVELS + 1, P), f)
    for n in range(LEVELS):
        masks[:, n] = ((i[:, None] >> (n + 1)) == (i[None] >> (n + 1))) & ((i[:, None] >> n) != (i[None] >> n))
    masks[:, LEVELS] = i[:, None] == i[None]
    t = np.arange(LAT)
    inv = (10000.0 ** (-np.arange(0, 32, 2, dtype=f) / 32)).astype(f)
    row, col = (t // GRID_W).astype(f), (t % GRID_W).astype(f)
    ang = np.concatenate([row[:, None] * inv] * 2 + [col[:, None] * inv] * 2, axis=1)
    rope = np.stack([np.tile(np.cos(ang).T, (2, 1)), np.tile(np.sin(ang).T, (2, 1))], axis=1).astype(f)
    rot = np.zeros((P, P), f)
    for m in range(P):
        rot[(m + 16, m) if m % 32 < 16 else (m - 16, m)] = -1.0 if m % 32 < 16 else 1.0
    tri = np.zeros((P, 3, P), np.float32)
    tri[:, 0] = np.where(i[None] >= i[:, None], 0.0, -1e30)
    tri[:, 1] = np.where(i[None] <= i[:, None], 0.0, -1e30)
    tri[:, 2] = np.eye(P)
    tri = tri.astype(ml_dtypes.bfloat16)

    arrays = {
        "small": small, "x": x, "ada": ada, "w": w, "ident": np.eye(P, dtype=f), "masks": masks.reshape(P, -1),
        "rope": rope, "rot": rot, "tri": tri,
    }
    arrays = {k: np.ascontiguousarray(v) for k, v in arrays.items()}
    nc = bacc.Bacc("TRN2", target_bir_lowering=False, num_devices=1)
    aps = [nc.dram_tensor(f"in_{n}", v.shape, mybir.dt.from_np(v.dtype), kind="ExternalInput").ap() for n, v in arrays.items()]
    out = nc.dram_tensor("out", (P, KC, LAT), F32, kind="ExternalOutput").ap()
    trunk(nc, *aps, out)
    r = run_bass_kernel_spmd(nc, [{f"in_{n}": v for n, v in arrays.items()}], core_ids=[0])
    y = r.results[0]["out"]
    return np.ascontiguousarray(y.transpose(2, 1, 0).reshape(1, LAT, D))
```

```python
from contextlib import ExitStack

import concourse.bass as bass
from concourse import mybir

F32 = mybir.dt.float32
F32R = mybir.dt.float32r
BF16 = mybir.dt.bfloat16
U8 = mybir.dt.uint8
ALU = mybir.AluOpType
ACT = mybir.ActivationFunctionType
AX = mybir.AxisListType

P = 128
D = 1024
KC = D // P
CTX, LAT = 256, 512
TOK = CTX + LAT
NCH = TOK // P
CCH = CTX // P
FF = 2816
FC = FF // P
GROUPS = (8, 8, 6)
HEADS = 8
GRID_H, GRID_W = LAT // 64, 64
EPS = 1e-6
LEVELS = 7
AT_SCALE = 64 ** -0.5
FWD = list(range(NCH))
BWD = list(range(CCH - 1, -1, -1)) + list(range(NCH - 1, CCH - 1, -1))
assert sum(GROUPS) == FC

PC0, PL0, PE0 = 512 - CTX, 512, 512 + LAT

T_HG, T_HGO = 0, 5 * HEADS
T_FF0 = T_HGO + KC
FF_TILES = 2 * FC + len(GROUPS) * KC
T_AT = T_FF0 + FF_TILES
T_ATO = T_AT + 12
T_FF1 = T_ATO + KC
TILES = T_FF1 + FF_TILES
ADA_GROUPS = 24
ADA_FIRST = 4
SH1, SC1, G1, SH2, SC2, G2 = range(6)

SMALL = {}
_at = 0
for _n, _w in (("c", 2 * KC), ("ada_b", 96), ("n1", 16), ("n2", 16), ("conv", 10 * (2 * FC + 1)),
               ("lb", 24), ("hgn", 1), ("bqkv", 12), ("sink", 16), ("fin", 8)):
    SMALL[_n] = (_at, _at + _w)
    _at += _w
NSMALL = _at


class Tally:

    def __init__(self):
        self.base, self.inner, self.loop = 0, 0, None

    def enter(self, i, per):
        self.base, self.inner, self.loop = self.base + self.inner, 0, (i, per)

    def leave(self, trips):
        assert self.inner == self.loop[1], (self.inner, self.loop[1])
        self.base, self.inner, self.loop = self.base + trips * self.inner, 0, None

    def add(self, n=1):
        self.inner += n
        return self

    def now(self, back=0):
        n = self.base + self.inner - back
        return n if self.loop is None else self.loop[0] * self.loop[1] + n

    def some(self, back=0):
        return self.base + self.inner - back > 0

    def times(self, m, plus):
        n = m * (self.base + self.inner) + plus
        return n if self.loop is None else self.loop[0] * (m * self.loop[1]) + n

    def half(self, back=0, unit=1):
        n = unit * ((self.base + self.inner - back + 1) // 2)
        if self.loop is None:
            return n
        assert self.loop[1] % 2 == 0
        return self.loop[0] * (self.loop[1] // 2 * unit) + n


def trunk(nc, small_in, x_in, ada_in, w_in, ident_in, masks_in, rope_in, rot_in, tri_in, out):
    ctx = ExitStack()
    with ctx:
        def sb(name, shape, dt=F32, scope=ctx):
            return scope.enter_context(nc.sbuf_tensor(name, shape, dt))

        def sem(name):
            return ctx.enter_context(nc.semaphore(name))

        X = sb("X", [P, KC, TOK])
        HH = sb("HH", [P, KC, TOK], F32R)
        HL = sb("HL", [P, KC, TOK], F32R)
        Y = sb("Y", [P, KC, TOK])
        WR = [sb(f"WR{i}", [P, KC, P]) for i in range(2)]
        WH = [sb(f"WH{i}", [P, KC, P], F32R) for i in range(2)]
        WL = [sb(f"WL{i}", [P, KC, P], F32R) for i in range(2)]
        AR = [sb(f"ada_raw{i}", [P, 512]) for i in range(2)]
        AH = [sb(f"ada_high{i}", [P, 512], F32R) for i in range(2)]
        AL = [sb(f"ada_low{i}", [P, 512], F32R) for i in range(2)]
        ident = sb("ident", [P, P])
        ones = sb("ones", [P, 1])
        eps_t = sb("eps_t", [P, 1])
        masks = sb("masks", [P, LEVELS + 1, P], U8)
        small = sb("small", [P, NSMALL])
        silu_c = sb("silu_c", [P, KC, 2])
        sig_c = sb("sig_c", [P, KC, 2])
        silu_p = sb("silu_p", [P, KC, 4], F32R)
        ada_row = sb("ada_row", [4, 512])
        fold = sb("fold", [4, 2])
        ada = sb("ada", [P, 96, 2])
        coef = sb("coef", [P, KC, 2])
        lbt = sb("lbt", [P, 4, HEADS])
        oml = sb("oml", [P, HEADS])
        lbv = sb("lbv", [P, HEADS])
        std6 = sb("std6", [P, NCH])
        rstd6 = sb("rstd6", [P, NCH])
        cw = [sb(f"cw{i}", [P, 10]) for i in range(2)]
        hold = sb("hold", [P, 1])
        hold_act = sb("hold_act", [P, 16])
        hold_pool = sb("hold_pool", [P, 4])

        def part(name):
            a, b = SMALL[name]
            return small[:, a:b]

        c_in = part("c").rearrange("p (k v) -> p k v", v=2)
        ada_b = part("ada_b")
        norm_g = {0: part("n1").rearrange("p (l k) -> p l k", l=2), 1: part("n2").rearrange("p (l k) -> p l k", l=2)}
        conv = part("conv").rearrange("p (n t) -> p n t", t=10)
        hgn = part("hgn")
        bqkv = part("bqkv")
        fin_g = part("fin")

        with ExitStack() as s:
            AD0 = sb("AD0", [P, ADA_FIRST, 4, 1024], F32, s)
        with ExitStack() as s:
            KF = [sb(f"KF{i}", [P, TOK], F32, s) for i in range(2)]
            KB = [sb(f"KB{i}", [P, TOK], F32, s) for i in range(2)]
            CF = [sb(f"CF{i}", [P, TOK], F32, s) for i in range(2)]
            CB = [sb(f"CB{i}", [P, TOK], F32, s) for i in range(2)]
            Q = [sb(f"Q{i}", [P, TOK], F32, s) for i in range(2)]
            VT = sb("VT", [P, TOK], F32, s)
            V = sb("V", [P, TOK], F32, s)
            RF = sb("RF", [P, TOK], F32, s)
            RB = sb("RB", [P, TOK], F32, s)
            QL = [sb(f"QL{i}", [P, TOK], F32, s) for i in range(2)]
            KL = [sb(f"KL{i}", [P, TOK], F32, s) for i in range(2)]
            PS = sb("PS", [P, TOK], F32, s)
            SF = sb("SF", [P, NCH - 1, P], F32, s)
            SB = sb("SB", [P, NCH - 1, P], F32, s)
            O1 = sb("O1", [P, TOK], F32, s)
            O2 = sb("O2", [P, TOK], F32, s)
            TF = sb("TF", [P, NCH], F32, s)
            TB = sb("TB", [P, NCH], F32, s)
        with ExitStack() as s:
            GH = sb("GH", [P, max(GROUPS), TOK], F32R, s)
            GL = sb("GL", [P, max(GROUPS), TOK], F32R, s)
            UW = (GRID_H + 2) * (GRID_W + 2)
            UP = [sb(f"UP{i}", [P, UW + CTX + 2], F32, s) for i in range(2)]
            ACC = [sb(f"ACC{i}", [P, TOK], F32, s) for i in range(2)]
        with ExitStack() as s:
            KT = sb("KT", [P, TOK], F32, s)
            AVT = sb("AVT", [P, TOK], F32, s)
            AV = sb("AV", [P, NCH, P], F32, s)
            QT = sb("QT", [P, 4, LAT], F32, s)
            RAW = [sb(f"RAW{i}", [P, LAT], F32, s) for i in range(2)]
            ROT = sb("ROT", [P, LAT], F32, s)
            PB = [sb(f"PB{i}", [P, 5 * P], F32, s) for i in range(3)]
            PT = [sb(f"PT{i}", [P, 5, 4, P], F32, s) for i in range(2)]
            rope = sb("rope", [P, 2, LAT], F32, s)
            rotm = sb("rotm", [P, P], F32, s)
            tri = sb("tri", [P, 3, P], BF16, s)
            nsink = sb("nsink", [P, 16], F32, s)
            mx = [sb(f"mx{i}", [P, 1], F32, s) for i in range(2)]
            nm = [sb(f"nm{i}", [P, 1], F32, s) for i in range(2)]
            den = [sb(f"den{i}", [P, 1], F32, s) for i in range(4)]
            es = [sb(f"es{i}", [P, 1], F32, s) for i in range(4)]
            den2 = [sb(f"den2{i}", [P, 1], F32, s) for i in range(2)]
            rden = [sb(f"rden{i}", [P, 1], F32, s) for i in range(2)]

        SLOT = [ctx.enter_context(nc.psum_tensor(f"slot{i}", [P, 1024], F32)) for i in range(2)]
        MA = ctx.enter_context(nc.psum_tensor("MA", [P, 1024], F32))
        MB = ctx.enter_context(nc.psum_tensor("MB", [P, 1024], F32))

        mask_stage = Y[:, 6:8, :].rearrange("p c t -> p (c t)")[:, 0:(LEVELS + 1) * P]
        SQ = [Y[:, 0, :], Y[:, 1, :]]
        SSQ = Y[:, 2, :]
        NT = [Y[:, 3, :], Y[:, 4, :]]

        small_in_done, x_in_done, const_done, rope_done = sem("small_in_done"), sem("x_in_done"), sem("const_done"), sem("rope_done")
        ada0_in = [sem(f"ada0_in{i}") for i in range(ADA_FIRST)]
        w_in_done = [sem(f"w_in_done{i}") for i in range(2)]
        piece_in = [sem(f"piece_in{i}") for i in range(2)]
        w_hi_done, w_split = sem("w_hi_done"), sem("w_split")
        tile_done = sem("tile_done")
        evacuated = [sem(f"evacuated{i}") for i in range(2)]
        piece_hi, piece_split = sem("piece_hi"), sem("piece_split")
        piece_used = sem("piece_used")
        sig_ready, silu_ready, lb_shifted = sem("sig_ready"), sem("silu_ready"), sem("lb_shifted")
        ada_summed, ada_copied, ada_turned, ada_ready = sem("ada_summed"), sem("ada_copied"), sem("ada_turned"), sem("ada_ready")
        sq_ready, sq_added = sem("sq_ready"), sem("sq_added")
        ss_ready, std_ready = sem("ss_ready"), sem("std_ready")
        rstd_ready, rstd_spread = sem("rstd_ready"), sem("rstd_spread")
        normed, hi_ready, lo_ready = sem("normed"), sem("hi_ready"), sem("lo_ready")
        dve_step = sem("dve_step")
        gate_sig = sem("gate_sig")
        level_ready, scores_done, scores_read = sem("level_ready"), sem("scores_done"), sem("scores_read")
        v_turned, v_ready = sem("v_turned"), sem("v_ready")
        kq_final, k_turned, kt_ready = sem("kq_final"), sem("k_turned"), sem("kt_ready")
        kv_done, states_ready = sem("kv_done"), sem("states_ready")
        early_hi, early_lo = sem("early_hi"), sem("early_lo")
        o_done, o_squared, o_evac, y_ready = sem("o_done"), sem("o_squared"), sem("o_evac"), sem("y_ready")
        conv_done, gelu_done, g_hi, g_lo = sem("conv_done"), sem("gelu_done"), sem("g_hi"), sem("g_lo")
        taps_ready = sem("taps_ready")
        rot_done, roped = sem("rot_done"), sem("roped")
        at_scores, row_max, probs_ready, probs_scaled = sem("at_scores"), sem("row_max"), sem("probs_ready"), sem("probs_scaled")
        p_turned, pt_ready, pv_done, at_out = sem("p_turned"), sem("pt_ready"), sem("pv_done"), sem("at_out")
        out_scaled, out_sent = sem("out_scaled"), sem("out_sent")

        def halves(t, s, which):
            return t[:, :].rearrange("p (n two s) -> p n two s", two=2, s=s)[:, :, which, :]

        def both(t, s, which, at):
            return halves(t, s, which)[:, :, at:at + 1].to_broadcast([P, TOK // (2 * s), s])

        def padded(u):
            return u[:, 0:UW].rearrange("p (h w) -> p h w", w=GRID_W + 2), u[:, UW:]

        def window(bi):
            first = max(bi - 1, 0)
            return first, min(bi + 1, LAT // P - 1) - first + 1

        UNITS = [(bi, half, r) for bi in range(LAT // P) for half in range(2) for r in range(4)]

        def spans(layer_tokens):
            lat = (slice(PL0, PE0), slice(CTX, TOK), 0)
            return [(slice(PC0, PL0), slice(0, CTX), 1), lat] if layer_tokens == TOK else [lat]

        def tile_pairs(loop, tile, first, end):
            def body(i):
                for s in range(2):
                    tile(s, i * 2 + (first + s))
            assert first % 2 == 0 and end % 2 == 0
            loop((end - first) // 2, 2, 0, body)

        def weights_to_attention(loop, tile, piece, last_head):
            def beside_head(parity, t, n):
                for j in range(5):
                    if j in (2, 3):
                        for k in range(2):
                            piece(k, n + 2 * (j - 2) + k)
                    tile((parity + j) % 2, t + j)

            for t in range(7):
                tile(t % 2, t)
            n0 = 4 * ADA_FIRST
            beside_head(1, 7, n0)

            def two_heads(i):
                beside_head(0, i * 10 + 12, i * 8 + (n0 + 4))
                beside_head(1, i * 10 + 17, i * 8 + (n0 + 8))
            loop(3, 10, 8, two_heads)
            n = n0 + 28
            for k in range(4):
                piece(k % 2, n + k)
                if k == 0:
                    last_head()
            t, n = 42, n + 4

            def one_each(trips):
                nonlocal t, n

                def body(i):
                    for j in range(4):
                        tile(j % 2, i * 4 + (t + j))
                        piece(j % 2, i * 4 + (n + j))
                if trips == 1:
                    body(0)
                else:
                    loop(trips, 4, 4, body)
                t, n = t + 4 * trips, n + 4 * trips

            def plain(tiles):
                nonlocal t
                tile_pairs(loop, tile, t, t + tiles)
                t += tiles

            plain(T_FF0 + 4 - t)
            for g, chunks in enumerate(GROUPS):
                one_each(chunks // 2 - (g == 0))
                if g < 2:
                    plain(2)
                    one_each(1)
                    plain(2)
            plain(KC)
            assert (t, n) == (T_AT, 4 * ADA_GROUPS)

        block = ctx.enter_context(nc.Block())

        @block.sync
        def _(sp):
            sp.dma_start(small[:, :], small_in).then_inc(small_in_done, 16)
            for g in range(ADA_FIRST):
                sp.dma_start(AD0[:, g, :, :], ada_in[4 * g:4 * g + 4].rearrange("n p f -> p n f")).then_inc(ada0_in[g], 16)
                if g == 0:
                    sp.dma_start(ident[:, :], ident_in).then_inc(const_done, 16)
                    sp.dma_start(mask_stage, masks_in).then_inc(const_done, 16)
                    sp.dma_start(X[:, :, :], x_in).then_inc(x_in_done, 16)

            split = Tally()
            raw = Tally()

            def load_tile(s, t):
                if split.some(1):
                    sp.wait_ge(w_split, split.now(1))
                split.add()
                sp.dma_start(WR[s][:, :, :], w_in[bass.ds(t, 1)].rearrange("o p k f -> p (o k) f")).then_inc(w_in_done[s], 16)

            def load_piece(_, n):
                for f in range(2):
                    if raw.some(1):
                        sp.wait_ge(piece_split, raw.now(1))
                    raw.add()
                    sp.dma_start(AR[f][:, :], ada_in[bass.ds(n, 1)][:, :, f * 512:(f + 1) * 512].rearrange("o p n -> p (o n)")).then_inc(piece_in[f], 16)

            def loop(trips, tiles, pieces, body):
                with nc.sync.Fori(0, trips) as i:
                    split.enter(i, tiles)
                    raw.enter(i, 2 * pieces)
                    body(i)
                    split.leave(trips)
                    raw.leave(trips)

            weights_to_attention(loop, load_tile, load_piece, lambda: None)
            for s in range(2):
                sp.wait_ge(evacuated[s], T_AT // 2)
            sp.dma_start(rope[:, :, :], rope_in).then_inc(rope_done, 16)
            sp.dma_start(rotm[:, :], rot_in).then_inc(rope_done, 16)
            sp.dma_start(tri[:, :, :], tri_in).then_inc(rope_done, 16)
            tile_pairs(loop, load_tile, T_AT, TILES)
            for c in range(KC):
                sp.wait_ge(out_scaled, c + 1)
                sp.dma_start(out[:, c, :], Y[:, c, CTX:TOK]).then_inc(out_sent, 16)
            sp.wait_ge(out_sent, 16 * KC)

        @block.gpsimd
        def _(pool):
            n, pieces = Tally(), Tally()

            def split_tile(s, _):
                n.add()
                pool.wait_ge(w_in_done[s], n.half(0, 16))
                if n.some(2):
                    pool.wait_ge(tile_done, n.now(2))
                pool.tensor_tensor(hold_pool[:, s:s + 1], ones[:, :], ones[:, :], ALU.subtract)
                pool.tensor_scalar(WH[s][:, :, :], WR[s][:, :, :], 1.0, 0.0, ALU.mult, ALU.add).then_inc(w_hi_done, 1)
                pool.wait_ge(w_hi_done, n.now())
                pool.tensor_tensor(WL[s][:, :, :], WR[s][:, :, :], WH[s][:, :, :].bitcast(F32), ALU.subtract).then_inc(w_split, 1)

            def split_piece(_, n):
                for f in range(2):
                    pieces.add()
                    pool.wait_ge(piece_in[f], pieces.half(0, 16))
                    if pieces.some(2):
                        pool.wait_ge(piece_used, pieces.now(2))
                    pool.tensor_tensor(hold_pool[:, 2 + f:3 + f], ones[:, :], ones[:, :], ALU.subtract)
                    pool.tensor_scalar(AH[f][:, :], AR[f][:, :], 1.0, 0.0, ALU.mult, ALU.add).then_inc(piece_hi, 1)
                    pool.wait_ge(piece_hi, pieces.now())
                    pool.tensor_tensor(AL[f][:, :], AR[f][:, :], AH[f][:, :].bitcast(F32), ALU.subtract).then_inc(piece_split, 1)

            def loop(trips, tiles, per, body):
                with nc.gpsimd.Fori(0, trips) as i:
                    n.enter(i, tiles)
                    pieces.enter(i, 2 * per)
                    body(i)
                    n.leave(trips)
                    pieces.leave(trips)

            def split_heads():
                pool.wait_ge(tile_done, T_HGO)
                for h in range(HEADS - 1):
                    pool.wait_ge(y_ready, h + 1)
                    pool.tensor_scalar(HH[:, h, :], Y[:, h, :], 1.0, 0.0, ALU.mult, ALU.add).then_inc(early_hi, 1)
                    pool.wait_ge(early_hi, h + 1)
                    pool.tensor_tensor(HL[:, h, :], Y[:, h, :], HH[:, h, :].bitcast(F32), ALU.subtract).then_inc(early_lo, 1)

            pool.wait_ge(lb_shifted, 1)
            weights_to_attention(loop, split_tile, split_piece, split_heads)
            tile_pairs(loop, split_tile, T_AT, TILES)
        @block.tensor
        def _(pe):
            mm = nc.tensor.matmul
            turn = nc.tensor.transpose
            tile, rows, pieces, stats, sums, parts = Tally(), Tally(), Tally(), Tally(), Tally(), Tally()

            def loop(trips, counts, body):
                with nc.tensor.Fori(0, trips) as i:
                    for t, per in counts:
                        t.enter(i, per)
                    body(i)
                    for t, _ in counts:
                        t.leave(trips)

            def chunk(c):
                return slice(PC0 + c * P, PC0 + (c + 1) * P)

            def begin_tile(s):
                tile.add()
                pe.wait_ge(w_split, tile.now())
                if tile.some(2):
                    pe.wait_ge(evacuated[s], tile.half(2))

            def products(s, half, k, hi, lo, kn=KC):
                po, to, _ = spans(TOK)[half]
                mm(SLOT[s][:, po], WH[s][:, k, :], hi[:, k, to], start=(k == 0), stop=False)
                mm(SLOT[s][:, po], WH[s][:, k, :], lo[:, k, to], start=False, stop=False)
                last = mm(SLOT[s][:, po], WL[s][:, k, :], hi[:, k, to], start=False, stop=(k == kn - 1))
                if half == 1 and k == kn - 1:
                    last.then_inc(tile_done, 1)

            def half_tile(s, half, hi, lo, kn=KC):
                for k in range(kn):
                    products(s, half, k, hi, lo, kn)

            def first_tiles(tokens, tokens1=None):
                for s in range(2):
                    begin_tile(s)
                done = parts.now()
                parts.add(KC)
                for k in range(KC):
                    pe.wait_ge(lo_ready, done + k + 1)
                    for s in range(2):
                        for half in range(2) if (tokens, tokens1 or tokens)[s] == TOK else (1,):
                            products(s, half, k, HH, HL)

            def full_tile(s, tokens, hi, lo, kn=KC):
                begin_tile(s)
                if tokens == TOK:
                    half_tile(s, 0, hi, lo, kn)
                half_tile(s, 1, hi, lo, kn)

            def more_tiles(pairs, tokens, hi, lo, kn=KC):
                def body(i):
                    full_tile(0, tokens, hi, lo, kn)
                    full_tile(1, tokens, hi, lo, kn)
                loop(pairs, [(tile, 2)], body)

            def ada_products(piece, k0, first, last):
                for k in range(2):
                    m = mm(MB[0:2, 0:512], silu_c[:, k0 + k, :], piece[:, k, :], start=(first and k == 0), stop=(last and k == 1))
                return m

            def ada_turn(n, add):
                pe.wait_ge(ada_copied, rows.now())
                if rows.some(1):
                    pe.wait_ge(ada_ready, rows.now(1))
                for m in range(4):
                    last = mm(MB[:, 512 + 2 * m:514 + 2 * m], ada_row[0:n, m * P:(m + 1) * P], add[0:n, 0:2], start=True, stop=True)
                last.then_inc(ada_turned, 1)

            def ada_piece(k):
                for f in range(2):
                    pieces.add()
                    pe.wait_ge(piece_split, pieces.now())
                    mm(MB[0:4, 0:512], silu_p[:, 2 * k + f, :], AH[f][:, :], start=(k == 0 and f == 0), stop=False)
                    mm(MB[0:4, 0:512], silu_p[:, 2 * k + f, :], AL[f][:, :], start=False, stop=(k == 3 and f == 1)).then_inc(piece_used, 1)
                if k == 3:
                    rows.add()

            def ada_tiles(trips, tokens, hi, lo, kn=KC):
                def body(i):
                    for j in range(4):
                        begin_tile(j % 2)
                        half_tile(j % 2, 0, hi, lo, kn)
                        ada_piece(j)
                        half_tile(j % 2, 1, hi, lo, kn)
                    ada_turn(4, fold)
                if trips == 1:
                    body(0)
                else:
                    loop(trips, [(tile, 4), (pieces, 8), (rows, 1)], body)

            pe.wait_ge(silu_ready, 3)
            pe.wait_ge(const_done, 32)
            for g in range(ADA_FIRST):
                pe.wait_ge(ada0_in[g], 16)
                for k in range(4):
                    last = ada_products(AD0[:, g, k, :].rearrange("p (k f) -> p k f", k=2), 2 * k, k == 0, k == 3)
                last.then_inc(ada_summed, 1)
                rows.add()
                ada_turn(2, ident)

            def token_sums(src, first):
                stats.add()
                for c in range(first, NCH):
                    last = mm(MA[:, c:c + 1], src[:, c * P:(c + 1) * P], ones[:, :], start=True, stop=True)
                last.then_inc(ss_ready, 1)

            def spread(first):
                pe.wait_ge(rstd_ready, stats.now())
                for c in range(first, NCH):
                    last = mm(MB[:, chunk(c)], rstd6[:, c:c + 1].to_broadcast([P, P]), ident[:, :], start=True, stop=True)
                last.then_inc(rstd_spread, 1)

            def norm_pe(first):
                sums.add(KC - 1)
                pe.wait_ge(sq_added, sums.now())
                pe.wait_ge(ada_ready, rows.now())
                token_sums(SSQ, first)
                spread(first)

            level, head = Tally(), Tally()

            def level_scores(b, n):
                level.add()
                pe.wait_ge(level_ready, level.now())
                if level.some(1):
                    pe.wait_ge(scores_read, level.now(1))
                q = QL[n % 2] if n < LEVELS else Q[b]
                for c in range(NCH):
                    t = slice(c * P, (c + 1) * P)
                    last = mm(MA[:, chunk(c)], KL[n % 2][:, t], q[:, t], start=True, stop=True)
                last.then_inc(scores_done, 1)

            def value_turn(b):
                for c in range(NCH):
                    last = turn(MB[:, chunk(c)], VT[:, c * P:(c + 1) * P], ident[:, :])
                last.then_inc(v_turned, 1)

            def key_value(b):
                pe.wait_ge(kq_final, head.now())
                pe.wait_ge(ada_ready, rows.now())
                pe.wait_ge(v_ready, head.now())
                for src, dst in ((KF, MB), (KB, MA)):
                    if dst is MA:
                        pe.wait_ge(scores_read, level.now())
                    for c in range(NCH):
                        last = turn(dst[:, chunk(c)], src[b][:, c * P:(c + 1) * P], ident[:, :])
                    last.then_inc(k_turned, 1)
                for n, (kt, dst, order) in enumerate(((RF, MB, FWD), (RB, MA, BWD))):
                    pe.wait_ge(kt_ready, head.times(2, n - 1))
                    for c in order[:-1]:
                        t = slice(c * P, (c + 1) * P)
                        last = mm(dst[:, chunk(c)], kt[:, t], V[:, t], start=True, stop=True)
                    last.then_inc(kv_done, 1)

            def outputs(b):
                pe.wait_ge(states_ready, head.times(2, 0))
                for c in range(NCH):
                    t = slice(c * P, (c + 1) * P)
                    f, k = FWD.index(c), BWD.index(c)
                    last = mm(MB[:, chunk(c)], V[:, t], PS[:, t], start=True, stop=(f == 0 and k == 0))
                    if f > 0:
                        last = mm(MB[:, chunk(c)], SF[:, f - 1, :], CF[b][:, t], start=False, stop=(k == 0))
                    if k > 0:
                        last = mm(MB[:, chunk(c)], SB[:, k - 1, :], CB[b][:, t], start=False, stop=True)
                last.then_inc(o_done, 1)

            def head_sums():
                pe.wait_ge(o_squared, head.now())
                token_sums(O2, 0)

            def head_spread():
                pe.wait_ge(o_evac, head.now())
                spread(0)

            def head_step(b, parity, tail=True, project=True):
                def between(n):
                    if tail and n == 0:
                        level_scores(1 - b, LEVELS)
                        key_value(1 - b)
                    if tail and n == 1:
                        outputs(1 - b)
                    if tail and n == 2:
                        head_sums()
                    if n == 3:
                        if tail:
                            head_spread()
                        level_scores(b, 0)
                    if n == 4:
                        if tail:
                            pe.wait_ge(y_ready, head.now())
                        head.add()
                        value_turn(b)
                    if n >= 4:
                        level_scores(b, n - 3)
                    if n == 5:
                        pe.wait_ge(v_ready, head.now())
                    if 5 <= n < 9:
                        ada_piece(n - 5)
                    if n == 9:
                        ada_turn(4, fold)

                for n in range(10):
                    if project:
                        s = (parity + n // 2) % 2
                        if n % 2 == 0:
                            begin_tile(s)
                        half_tile(s, n % 2, HH, HL)
                    elif 2 <= n < HEADS + 1:
                        pe.wait_ge(early_lo, n - 1)
                        head_products(n - 2)
                    between(n)

            def head_products(k):
                for s in range(2):
                    for half in range(2):
                        products(s, half, k, HH, HL)

            norm_pe(0)
            first_tiles(TOK)
            for j in range(2, 5):
                full_tile(j % 2, TOK, HH, HL)
            head_step(0, 1, tail=False)

            def two_heads(i):
                head_step(1, 0)
                head_step(0, 1)
            loop(3, [(tile, 10), (rows, 2), (pieces, 16), (level, 16), (head, 2), (stats, 2)], two_heads)
            for s in range(2):
                pe.wait_ge(evacuated[s], T_HGO // 2)
            for s in range(2):
                begin_tile(s)
            head_step(1, 0, project=False)
            level_scores(1, LEVELS)
            key_value(1)
            outputs(1)
            head_sums()
            head_spread()
            parts.add(1)
            pe.wait_ge(lo_ready, parts.now())
            head_products(HEADS - 1)
            more_tiles(KC // 2 - 1, TOK, HH, HL)

            gated = Tally()

            def feed_forward(tokens, layer):
                gated.add(2)
                for g, n in enumerate(GROUPS):
                    if g == 0:
                        first_tiles(tokens)
                    if layer == 0:
                        if g == 0:
                            more_tiles(1, tokens, HH, HL)
                        ada_tiles(n // 2 - (g == 0), tokens, HH, HL)
                    else:
                        more_tiles(n - (g == 0), tokens, HH, HL)
                    gated.add(n)
                    begin_tile(0)
                    for k in range(n):
                        if k in (0, n - 1):
                            pe.wait_ge(g_lo, gated.now(k == 0))
                        for half in range(2) if tokens == TOK else (1,):
                            products(0, half, k, GH, GL, n)
                    full_tile(1, tokens, GH, GL, n)
                    if layer == 0 and g < 2:
                        ada_tiles(1, tokens, GH, GL, n)
                        more_tiles(1, tokens, GH, GL, n)
                    else:
                        more_tiles(KC // 2 - 1, tokens, GH, GL, n)

            norm_pe(0)
            feed_forward(TOK, 0)

            norm_pe(0)
            pe.wait_ge(rope_done, 48)
            rot, unit, block_n, vals = Tally(), Tally(), Tally(), Tally()
            vals.base = HEADS
            rot.base = 2

            def rotate(b, s, back=0):
                pe.wait_ge(evacuated[s], tile.half(back))
                rot.add()
                pe.wait_ge(roped, rot.now(1))
                mm(MA[:, 0:LAT], rotm[:, :], RAW[b][:, :], start=True, stop=True).then_inc(rot_done, 1)

            def at_score(u, bi, half, r):
                hp = slice(64 * half, 64 * half + 64)
                S = (MB, MA)[u % 2]
                first, n = window(bi)
                if u >= 2:
                    pe.wait_ge(probs_ready, unit.times(1, (u - 1)))
                q = QT[hp, r, bi * P:(bi + 1) * P]
                mm(S[:, PC0:PL0], q, KT[hp, 0:CTX], start=True, stop=True)
                edges = ([(0, 0)] if bi > 0 else []) + ([(n - 1, 1)] if bi < LAT // P - 1 else [])
                mm(S[:, PL0:PL0 + n * P], q, KT[hp, CTX + first * P:CTX + (first + n) * P], start=True, stop=False)
                for e, (at, which) in enumerate(edges):
                    last = mm(S[:, PL0 + at * P:PL0 + (at + 1) * P], tri[:, 2, :], tri[:, which, :], start=False, stop=(e == len(edges) - 1))
                last.then_inc(at_scores, 1)

            def at_turn(u, bi, half, r):
                pe.wait_ge(probs_scaled, unit.times(1, (u + 1)))
                if u >= 1:
                    pe.wait_ge(pt_ready, unit.times(1, u))
                for c in range(2 + window(bi)[1]):
                    last = turn(SLOT[0][:, chunk(c)], PB[u % 3][:, c * P:(c + 1) * P], ident[:, :])
                last.then_inc(p_turned, 1)

            def at_values(v, bi, half):
                first, n = window(bi)
                pe.wait_ge(pt_ready, unit.times(1, (4 * v + 4)))
                if half == 0 and bi > 0:
                    pe.wait_ge(at_out, block_n.times(1, bi))
                for j, c in enumerate([0, 1] + [CCH + first + j for j in range(n)]):
                    last = mm(SLOT[1][64 * half:64 * half + 64, 0:512], AV[:, c, 64 * half:64 * half + 64],
                              PT[v % 2][:, j, :, :].rearrange("p r q -> p (r q)"), start=(j == 0), stop=(j == n + 1))
                last.then_inc(pv_done, 1)

            def two_key_heads(i):
                first_tiles(TOK, LAT)
                parts.inner -= KC
                rotate(0, 0, 1)
                for r in range(1, 4):
                    full_tile((r + 1) % 2, LAT, HH, HL)
                    rotate(r % 2, r % 2, 1)
                begin_tile(1)
                half_tile(1, 0, HH, HL)
                rotate(0, 0, 1)
                half_tile(1, 1, HH, HL)
                at_score(0, *UNITS[0])
                pe.wait_ge(roped, rot.now())
                at_score(1, *UNITS[1])
                pe.wait_ge(evacuated[1], tile.half())
                for c in range(NCH):
                    last = turn(SLOT[0][:, chunk(c)], AVT[:, c * P:(c + 1) * P], ident[:, :])
                last.then_inc(v_turned, 1)
                at_score(2, *UNITS[2])
                vals.add()
                pe.wait_ge(v_ready, vals.now())
                for u in range(len(UNITS)):
                    if u + 3 < len(UNITS):
                        at_score(u + 3, *UNITS[u + 3])
                    if u % 4 == 0 and u:
                        at_values(u // 4 - 1, *UNITS[u - 1][:2])
                    at_turn(u, *UNITS[u])
                at_values(7, *UNITS[-1][:2])
                unit.add(len(UNITS))
                block_n.add(LAT // P)
                pe.wait_ge(at_out, block_n.now())

            loop(2, [(tile, 6), (rot, 5), (unit, 32), (block_n, 4), (vals, 1)], two_key_heads)
            parts.add(KC)
            first_tiles(LAT)
            more_tiles(KC // 2 - 1, LAT, HH, HL)
            norm_pe(CCH)
            feed_forward(LAT, 1)
            norm_pe(CCH)

        @block.scalar
        def _(act):
            go = nc.scalar.activation
            tile, squares, norms, stats = Tally(), Tally(), Tally(), Tally()
            his, added = Tally(), Tally()

            def loop(trips, counts, body):
                with nc.scalar.Fori(0, trips) as i:
                    for t, per in counts:
                        t.enter(i, per)
                    body(i)
                    for t, _ in counts:
                        t.leave(trips)

            def next_tile():
                tile.add()
                act.wait_ge(tile_done, tile.now())

            act.wait_ge(small_in_done, 16)
            go(sig_c[:, :, :], c_in, ACT.Sigmoid).then_inc(sig_ready, 1)
            act.wait_ge(lb_shifted, 1)
            go(lbt[:, 0:3, :], lbt[:, 0:3, :], ACT.Exp).then_inc(sig_ready, 1)

            def carry(n):
                go(hold_act[:, n:n + 1], hold_act[:, n:n + 1], ACT.Copy)

            def token_std(scale, first):
                stats.add()
                act.wait_ge(ss_ready, stats.now())
                go(std6[:, first:NCH], MA[:, first:NCH], ACT.Sqrt, bias=eps_t[:, :], scale=scale).then_inc(std_ready, 1)

            def norm_act(tokens, shift, tiles=None):
                t = slice(TOK - tokens, TOK)
                for c in range(KC):
                    if tiles is not None:
                        act.wait_ge(evacuated[c % 2], tiles // 2 + c // 2 + 1)
                    if c >= 2:
                        act.wait_ge(sq_added, added.now() + max(1, c - 2))
                    go(SQ[c % 2][:, t], X[:, c, t], ACT.Square).then_inc(sq_ready, 1)
                added.add(KC - 1)
                token_std(1.0 / D, (TOK - tokens) // P)
                if shift is None:
                    return
                for c in range(KC):
                    norms.add()
                    act.wait_ge(normed, norms.now())
                    for _, to, v in spans(tokens):
                        last = go(HH[:, c, to], NT[c % 2][:, to], ACT.Identity, bias=ada[:, shift + c, v:v + 1])
                    last.then_inc(hi_ready, 1)

            def ada_copy():
                rows.add()
                act.wait_ge(piece_used, rows.times(8, -8 * ADA_FIRST))
                go(ada_row[:, :], MB[0:4, 0:512], ACT.Copy).then_inc(ada_copied, 1)

            rows = Tally()
            rows.base = ADA_FIRST

            def mixer_hi(tokens, first=0):
                t = slice(TOK - tokens, TOK)
                for c in range(first, KC):
                    go(HH[:, c, t], Y[:, c, t], ACT.Copy).then_inc(hi_ready, 1)

            head = Tally()

            def decays(c, k, s):
                next_tile()
                go(c[:, :], SLOT[s][:, PC0:PE0], ACT.Sigmoid)
                go(k[:, :], SLOT[s][:, PC0:PE0], ACT.Sigmoid, scale=-1.0).then_inc(evacuated[s], 1)

            def query(b, s, h):
                next_tile()
                carry(b)
                go(Q[b][:, :], SLOT[s][:, PC0:PE0], ACT.Copy, scale=oml[:, bass.ds(h, 1)]).then_inc(evacuated[s], 1)

            def values(s):
                next_tile()
                go(VT[:, :], SLOT[s][:, PC0:PE0], ACT.Copy).then_inc(evacuated[s], 1)

            def gate(s, h):
                next_tile()
                carry(2 + s)
                go(Y[:, bass.ds(h, 1), :].rearrange("p o t -> p (o t)"), SLOT[s][:, PC0:PE0], ACT.Sigmoid).then_inc(gate_sig, 1)

            def value_copy(b):
                act.wait_ge(v_turned, head.now())
                go(V[:, :], MB[:, PC0:PE0], ACT.Copy).then_inc(v_ready, 1)

            def key_copies():
                for n, (dst, src) in enumerate(((RF, MB), (RB, MA))):
                    act.wait_ge(k_turned, head.times(2, n - 1))
                    go(dst[:, :], src[:, PC0:PE0], ACT.Copy).then_inc(kt_ready, 1)

            def output_copies():
                act.wait_ge(o_done, head.now())
                go(O2[:, :], MB[:, PC0:PE0], ACT.Square).then_inc(o_squared, 1)
                go(O1[:, :], MB[:, PC0:PE0], ACT.Copy, scale=hgn).then_inc(o_evac, 1)

            def head_step(b, parity, h, tail=True, project=True):
                s = parity
                if tail:
                    key_copies()
                    output_copies()
                if project:
                    decays(CF[1 - b], KF[1 - b], s)
                if tail:
                    token_std(1.0 / P, 0)
                if project:
                    decays(CB[1 - b], KB[1 - b], 1 - s)
                head.add()
                value_copy(b)
                if project:
                    query(1 - b, s, h + 1)
                    values(1 - s)
                ada_copy()
                if project:
                    gate(s, h + 1)

            act.wait_ge(x_in_done, 16)
            norm_act(TOK, SH1 * KC)
            decays(CF[0], KF[0], 0)
            decays(CB[0], KB[0], 1)
            query(0, 0, 0)
            values(1)
            gate(0, 0)
            head_step(0, 1, 0, tail=False)

            def two_heads(i):
                head_step(1, 0, i * 2 + 1)
                head_step(0, 1, i * 2 + 2)
            loop(3, [(tile, 10), (head, 2), (stats, 2), (rows, 2)], two_heads)
            head_step(1, 0, 7, project=False)
            key_copies()
            output_copies()
            token_std(1.0 / P, 0)
            act.wait_ge(y_ready, HEADS)
            mixer_hi(TOK, HEADS - 1)
            tile.add(KC)

            def feed_forward(tokens, layer):
                freed.add(2)
                def body(i, adds):
                    for b in range(2):
                        next_tile()
                        act.wait_ge(g_lo, freed.now(1))
                        freed.add()
                        conv_n.add()
                        act.wait_ge(taps_ready, conv_n.now())
                        lat, cx = padded(UP[b])
                        go(lat[:, 1:1 + GRID_H, 1:1 + GRID_W], SLOT[0][:, PL0:PE0].rearrange("p (h w) -> p h w", w=GRID_W), ACT.Copy)
                        if tokens == TOK:
                            go(cx[:, 1:1 + CTX], SLOT[0][:, PC0:PL0], ACT.Copy)
                        t0 = TOK - tokens
                        go(ACC[b][:, t0:TOK], SLOT[0][:, PE0 - tokens:PE0], ACT.Identity, scale=cw[b][:, 4:5], bias=cw[b][:, 9:10]).then_inc(evacuated[0], 1)
                        tile.add()
                        if b == 1 and adds:
                            ada_copy()
                        act.wait_ge(conv_done, conv_n.now())
                        go(ACC[b][:, t0:TOK], ACC[b][:, t0:TOK], ACT.Gelu).then_inc(gelu_done, 1)
                        act.wait_ge(evacuated[1], tile.half())
                        carry(4 + b)
                        go(GH[:, bass.ds(i * 2 + b, 1), t0:TOK].rearrange("p o t -> p (o t)"), ACC[b][:, t0:TOK], ACT.Copy).then_inc(g_hi, 1)

                for g, n in enumerate(GROUPS):
                    peel = int(layer == 0 and g == 0)
                    adds = int(layer == 0)
                    if peel:
                        body(0, False)
                    loop(n // 2 - peel, [(tile, 4), (conv_n, 2), (freed, 2), (rows, adds)], lambda i: body(i + peel, adds))
                    tile.add(KC)
                    if adds and g < 2:
                        ada_copy()

            conv_n, freed = Tally(), Tally()
            norm_act(TOK, SH2 * KC, T_HGO)
            feed_forward(TOK, 0)
            norm_act(TOK, 48 + SH1 * KC, T_AT - KC)

            rot, unit, pair = Tally(), Tally(), Tally()

            def at_exp(u, i, half, r):
                hd = bass.ds(i * 8 + (half * 4 + r), 1)
                S = (MB, MA)[u % 2]
                n = 2 + window(UNITS[u][0])[1]
                act.wait_ge(row_max, unit.times(1, (u + 1)))
                if u >= 3:
                    act.wait_ge(p_turned, unit.times(1, (u - 2)))
                go(PB[u % 3][:, 0:n * P], S[:, PC0:PC0 + n * P], ACT.Exp, scale=AT_SCALE, bias=nm[u % 2][:, :], accum_out=den[u % 4][:, :])
                go(es[u % 4][:, :], nsink[:, hd], ACT.Exp, scale=-1.0, bias=nm[u % 2][:, :]).then_inc(probs_ready, 1)

            def at_copy(u):
                bi, half, r = UNITS[u]
                n = 2 + window(bi)[1]
                v = u // 4
                act.wait_ge(p_turned, unit.times(1, (u + 1)))
                if v >= 2 and r == 0:
                    act.wait_ge(pv_done, pair.times(1, (v - 1)))
                go(PT[v % 2][:, 0:n, r, :], SLOT[0][:, PC0:PC0 + n * P].rearrange("p (n q) -> p n q", q=P), ACT.Copy).then_inc(pt_ready, 1)

            def two_key_heads(i):
                def raw(b, s, j):
                    act.wait_ge(roped, rot.now(1))
                    rot.add()
                    carry(6 + j)
                    go(RAW[b][:, :], SLOT[s][:, PL0:PE0], ACT.Identity, bias=bqkv[:, bass.ds(i * 6 + j, 1)]).then_inc(evacuated[s], 1)
                next_tile()
                carry(12)
                go(KT[:, 0:CTX], SLOT[0][:, PC0:PL0], ACT.Identity, bias=bqkv[:, bass.ds(i * 6, 1)])
                raw(0, 0, 0)
                for r in range(4):
                    next_tile()
                    raw((r + 1) % 2, (r + 1) % 2, 1 + r)
                next_tile()
                carry(13)
                go(AVT[:, :], SLOT[1][:, PC0:PE0], ACT.Identity, bias=bqkv[:, bass.ds(i * 6 + 5, 1)]).then_inc(evacuated[1], 1)
                at_exp(0, i, *UNITS[0][1:])
                at_exp(1, i, *UNITS[1][1:])
                vals.add()
                act.wait_ge(v_turned, vals.now())
                go(AV[:, :, :], SLOT[0][:, PC0:PE0].rearrange("p (c f) -> p c f", f=P), ACT.Copy).then_inc(v_ready, 1)
                at_exp(2, i, *UNITS[2][1:])
                for u in range(len(UNITS)):
                    at_copy(u)
                    if u + 3 < len(UNITS):
                        at_exp(u + 3, i, *UNITS[u + 3][1:])
                unit.add(len(UNITS))
                pair.add(8)

            vals = Tally()
            vals.base, rot.base = HEADS, 2
            loop(2, [(tile, 6), (rot, 5), (unit, 32), (pair, 8), (vals, 1)], two_key_heads)
            act.wait_ge(at_out, 8)
            mixer_hi(LAT)
            tile.add(KC)
            norm_act(LAT, 48 + SH2 * KC, T_ATO)
            feed_forward(LAT, 1)
            norm_act(LAT, None, TILES - KC)

        @block.vector
        def _(dve):
            tt, ts, stt, cp = nc.vector.tensor_tensor, nc.vector.tensor_scalar, nc.vector.scalar_tensor_tensor, nc.vector.tensor_copy
            tile, steps, rows, stats = Tally(), Tally(), Tally(), Tally()
            squares, added, his, spreads = Tally(), Tally(), Tally(), Tally()

            def loop(trips, counts, body):
                with nc.vector.Fori(0, trips) as i:
                    for t, per in counts:
                        t.enter(i, per)
                    body(i)
                    for t, _ in counts:
                        t.leave(trips)

            def mark(ins):
                steps.add()
                ins.then_inc(dve_step, 1)

            def settle():
                dve.wait_ge(dve_step, steps.now())

            def link(ins):
                mark(ins)
                settle()

            mark(nc.vector.memset(ones[:, :], 1.0))
            mark(nc.vector.memset(eps_t[:, :], EPS))
            mark(nc.vector.memset(hold[:, :], 0.0))
            mark(nc.vector.memset(hold_act[:, :], 0.0))
            dve.wait_ge(small_in_done, 16)
            lb = part("lb").rearrange("p (l h) -> p l h", l=3)
            link(tt(lbt[:, 3, :], lb[:, 0, :], lb[:, 1, :], ALU.max))
            link(tt(lbt[:, 3, :], lbt[:, 3, :], lb[:, 2, :], ALU.max))
            for n in range(3):
                last = tt(lbt[:, n, :], lb[:, n, :], lbt[:, 3, :], ALU.subtract)
            last.then_inc(lb_shifted, 1)
            dve.wait_ge(sig_ready, 1)
            tt(silu_c[:, :, :], c_in, sig_c[:, :, :], ALU.mult).then_inc(silu_ready, 1)
            dve.wait_ge(silu_ready, 1)
            link(cp(silu_p[:, :, 0:2], silu_c[:, :, :]))
            tt(silu_p[:, :, 2:4], silu_c[:, :, :], silu_p[:, :, 0:2].bitcast(F32), ALU.subtract).then_inc(silu_ready, 1)
            dve.wait_ge(const_done, 32)
            tt(fold[:, :], ident[0:4, 0:2], ident[0:4, 2:4], ALU.add).then_inc(silu_ready, 1)
            dve.wait_ge(sig_ready, 2)
            link(tt(lbt[:, 3, :], lbt[:, 0, :], lbt[:, 1, :], ALU.add))
            link(tt(lbt[:, 3, :], lbt[:, 3, :], lbt[:, 2, :], ALU.add))
            link(nc.vector.reciprocal(lbt[:, 3, :], lbt[:, 3, :]))
            link(tt(lbv[:, :], lbt[:, 0, :], lbt[:, 3, :], ALU.mult))
            link(ts(oml[:, :], lbv[:, :], -1.0, 1.0, ALU.mult, ALU.add))

            def ada_copy():
                rows.add()
                dve.wait_ge(ada_summed, rows.now())
                cp(ada_row[0:2, :], MB[0:2, 0:512]).then_inc(ada_copied, 1)

            def ada_add(j):
                dve.wait_ge(ada_turned, rows.now())
                tt(ada[:, bass.ds(j, 4), :], MB[:, 512:520].rearrange("p (m v) -> p m v", v=2),
                   ada_b[:, bass.ds(j, 4)].unsqueeze(2).to_broadcast([P, 4, 2]), ALU.add).then_inc(ada_ready, 1)

            def add_square(c, tokens):
                t = slice(TOK - tokens, TOK)
                if c == 0:
                    return
                dve.wait_ge(sq_ready, squares.now() + c + 1)
                if c > 1:
                    dve.wait_ge(sq_added, added.now())
                added.add()
                tt(SSQ[:, t], SQ[0][:, t] if c == 1 else SSQ[:, t], SQ[c % 2][:, t], ALU.add).then_inc(sq_added, 1)

            for g in range(ADA_FIRST):
                ada_copy()
                ada_add(4 * g)
                add_square(2 * g, TOK)
                add_square(2 * g + 1, TOK)

            def token_rstd(first):
                stats.add()
                dve.wait_ge(std_ready, stats.now())
                nc.vector.reciprocal(rstd6[:, first:NCH], std6[:, first:NCH]).then_inc(rstd_ready, 1)

            def norm_dve(tokens, gain, scale, shift):
                t = slice(TOK - tokens, TOK)
                squares.add(KC)
                if scale is not None:
                    dve.wait_ge(ada_ready, rows.now())
                    link(stt(coef[:, :, :], ada[:, scale:scale + KC, :], 1.0, gain.unsqueeze(2).to_broadcast([P, KC, 2]), ALU.add, ALU.mult))
                token_rstd((TOK - tokens) // P)
                dve.wait_ge(rstd_spread, stats.now())
                if scale is None:
                    for c in range(KC):
                        stt(Y[:, c, t], X[:, c, t], gain[:, c:c + 1], MB[:, PL0:PE0], ALU.mult, ALU.mult).then_inc(out_scaled, 1)
                    return

                lows = his.base + his.inner

                def scaled(c):
                    if c >= 2:
                        dve.wait_ge(lo_ready, lows + c - 1)
                    for po, to, v in spans(tokens):
                        last = stt(NT[c % 2][:, to], X[:, c, to], coef[:, c, v:v + 1], MB[:, po], ALU.mult, ALU.mult)
                    last.then_inc(normed, 1)

                def low(c):
                    his.add()
                    dve.wait_ge(hi_ready, his.now())
                    for _, to, v in spans(tokens):
                        last = stt(HL[:, c, to], NT[c % 2][:, to], ada[:, shift + c, v:v + 1], HH[:, c, to].bitcast(F32), ALU.add, ALU.subtract)
                    last.then_inc(lo_ready, 1)
                scaled(0)
                for c in range(KC):
                    if c + 1 < KC:
                        scaled(c + 1)
                    low(c)

            def mixer_lo(tokens, first=0):
                t = slice(TOK - tokens, TOK)
                for c in range(first, KC):
                    his.add()
                    dve.wait_ge(hi_ready, his.now())
                    tt(HL[:, c, t], Y[:, c, t], HH[:, c, t].bitcast(F32), ALU.subtract).then_inc(lo_ready, 1)

            def residual(tokens, gate):
                def body(i):
                    for s in range(2):
                        tile.add()
                        dve.wait_ge(tile_done, tile.now())
                        for po, to, v in spans(tokens):
                            x = X[:, bass.ds(i * 2 + s, 1), to].rearrange("p o t -> p (o t)")
                            g = ada[:, bass.ds(i * 2 + (gate + s), 1), v:v + 1].rearrange("p o v -> p (o v)")
                            last = stt(x, SLOT[s][:, po], g, x, ALU.mult, ALU.add)
                        last.then_inc(evacuated[s], 1)
                loop(KC // 2, [(tile, 2)], body)

            def last_residual(tokens, gate):
                for c in range(KC):
                    tile.add()
                    dve.wait_ge(tile_done, tile.now())
                    for po, to, v in spans(tokens):
                        last = stt(X[:, c, to], SLOT[c % 2][:, po], ada[:, gate + c, v:v + 1], X[:, c, to], ALU.mult, ALU.add)
                    last.then_inc(evacuated[c % 2], 1)
                    if c > 0:
                        add_square(c - 1, tokens)
                add_square(KC - 1, tokens)

            head, level = Tally(), Tally()

            def forget(b, parity, h):
                tile.add(2)
                dve.wait_ge(evacuated[parity], tile.half())
                tile.add()
                dve.wait_ge(evacuated[1 - parity], tile.half())
                tile.add(2)
                for c in (CF, CB):
                    mark(ts(c[b][:, :], c[b][:, :], oml[:, bass.ds(h, 1)], lbv[:, bass.ds(h, 1)], ALU.mult, ALU.add))
                settle()

            def products(b, n):
                s = 2 ** n
                level.add()
                q, k = QL[n % 2], KL[n % 2]
                tt(halves(q, s, 1), halves(Q[b], s, 1), halves(CF[b], s, 1), ALU.mult)
                tt(halves(q, s, 0), halves(Q[b], s, 0), halves(CB[b], s, 0), ALU.mult)
                if n == 0:
                    cp(halves(k, s, 0), halves(KF[b], s, 0))
                    cp(halves(k, s, 1), halves(KB[b], s, 1)).then_inc(level_ready, 1)
                else:
                    tt(halves(k, s, 0), halves(KF[b], s, 0), halves(RF, s, 0), ALU.mult)
                    tt(halves(k, s, 1), halves(KB[b], s, 1), halves(RB, s, 1), ALU.mult).then_inc(level_ready, 1)

            def diagonal(b):
                level.add()
                tt(KL[1][:, :], KF[b][:, :], KB[b][:, :], ALU.add).then_inc(level_ready, 1)

            def double(b, n):
                s = 2 ** n
                dve.wait_ge(level_ready, level.now())
                if n == 0:
                    mark(nc.vector.memset(halves(RF, s, 1), 1.0))
                    mark(nc.vector.memset(halves(RB, s, 0), 1.0))
                    mark(cp(halves(RF, s, 0), halves(CF[b], s, 1)))
                    mark(cp(halves(RB, s, 1), halves(CB[b], s, 0)))
                else:
                    mark(tt(halves(RF, s, 0), halves(RF, s, 0), both(CF[b], s, 1, s - 1), ALU.mult))
                    mark(tt(halves(RB, s, 1), halves(RB, s, 1), both(CB[b], s, 0, 0), ALU.mult))
                settle()
                mark(tt(halves(CF[b], s, 1), halves(CF[b], s, 1), both(CF[b], s, 0, s - 1), ALU.mult))
                mark(tt(halves(CB[b], s, 0), halves(CB[b], s, 0), both(CB[b], s, 1, 0), ALU.mult))
                settle()

            def take(n, back):
                dve.wait_ge(scores_done, level.now(back))
                if level.some(back + 1):
                    dve.wait_ge(scores_read, level.now(back + 1))
                mark(nc.vector.memset(hold[:, :], 0.0))
                for c in range(2):
                    t = slice(c * TOK // 2, (c + 1) * TOK // 2)
                    last = nc.vector.copy_predicated(
                        PS[:, t].rearrange("p (c t) -> p c t", t=P), masks[:, n:n + 1, :].to_broadcast([P, NCH // 2, P]),
                        MA[:, PC0 + t.start:PC0 + t.stop].rearrange("p (c t) -> p c t", t=P))
                last.then_inc(scores_read, 1)

            def finals(b):
                mark(cp(TF[:, :], CF[b][:, :].rearrange("p (c t) -> p c t", t=P)[:, :, P - 1:P].rearrange("p c o -> p (c o)")))
                mark(cp(TB[:, :], CB[b][:, :].rearrange("p (c t) -> p c t", t=P)[:, :, 0:1].rearrange("p c o -> p (c o)")))
                settle()
                mark(tt(CF[b][:, :], CF[b][:, :], Q[b][:, :], ALU.mult))
                mark(tt(CB[b][:, :], CB[b][:, :], Q[b][:, :], ALU.mult))
                tt(KF[b][:, :], KF[b][:, :], RF[:, :], ALU.mult)
                tt(KB[b][:, :], KB[b][:, :], RB[:, :], ALU.mult).then_inc(kq_final, 1)

            def states():
                settle()
                for n, (st, total, src, order) in enumerate(((SF, TF, MB, FWD), (SB, TB, MA, BWD))):
                    dve.wait_ge(kv_done, head.times(2, n - 1))
                    for j, c in enumerate(order[:-1]):
                        kv = src[:, PC0 + c * P:PC0 + (c + 1) * P]
                        if j == 0:
                            ins = cp(st[:, 0, :], kv)
                        else:
                            ins = stt(st[:, j, :], st[:, j - 1, :], total[:, c:c + 1], kv, ALU.mult, ALU.add)
                        if j < NCH - 2:
                            link(ins)
                    ins.then_inc(states_ready, 1)

            def head_out(h):
                dve.wait_ge(rstd_spread, stats.now())
                link(tt(O1[:, :], O1[:, :], MB[:, PC0:PE0], ALU.mult))
                y = Y[:, bass.ds(h, 1), :].rearrange("p o t -> p (o t)")
                tt(y, y, O1[:, :], ALU.mult).then_inc(y_ready, 1)

            def gate(s, h):
                dve.wait_ge(gate_sig, gates.add().now())
                y = Y[:, bass.ds(h, 1), :].rearrange("p o t -> p (o t)")
                tt(y, y, SLOT[s][:, PC0:PE0], ALU.mult).then_inc(evacuated[s], 1)

            gates = Tally()

            def head_step(b, parity, h, j0, tail=True, project=True):
                forget(b, parity, h)
                if tail:
                    take(LEVELS, 0)
                products(b, 0)
                if tail:
                    states()
                double(b, 0)
                products(b, 1)
                if tail:
                    token_rstd(0)
                    head_out(h - 1)
                head.add()
                take(0, 1)
                for n in range(2, LEVELS):
                    double(b, n - 1)
                    products(b, n)
                    take(n - 1, 1)
                diagonal(b)
                double(b, LEVELS - 1)
                finals(b)
                take(LEVELS - 1, 1)
                rows.add()
                ada_add(j0)
                if project:
                    gate(parity, h + 1)

            norm_dve(TOK, norm_g[0][:, 0, :], SC1 * KC, SH1 * KC)
            dve.wait_ge(const_done, 32)
            mark(cp(masks[:, :, :].rearrange("p n t -> p (n t)"), mask_stage))
            link(nc.vector.memset(PS[:, :], 0.0))
            gate(0, 0)
            j0 = 4 * ADA_FIRST
            head_step(0, 1, 0, j0, tail=False)

            def two_heads(i):
                head_step(1, 0, i * 2 + 1, i * 8 + (j0 + 4))
                head_step(0, 1, i * 2 + 2, i * 8 + (j0 + 8))
            loop(3, [(tile, 10), (rows, 2), (level, 16), (head, 2), (stats, 2), (gates, 2), (steps, 2 * 53)], two_heads)
            head_step(1, 0, 7, j0 + 28, project=False)
            take(LEVELS, 0)
            states()
            token_rstd(0)
            head_out(7)
            mixer_lo(TOK, HEADS - 1)
            last_residual(TOK, G1 * KC)
            norm_dve(TOK, norm_g[1][:, 0, :], SC2 * KC, SH2 * KC)

            conv_n = Tally()

            def feed_forward(tokens, layer):
                t0 = TOK - tokens
                for b in range(2):
                    nc.vector.memset(UP[b][:, :], 0.0).then_inc(g_lo, 1)
                n0 = layer * FC
                if layer == 0:
                    cp(cw[0][:, :], conv[:, 0, :]).then_inc(taps_ready, 1)
                def body(i, adds, col=None):
                    for b in range(2):
                        tile.add()
                        dve.wait_ge(evacuated[0], tile.half())
                        conv_n.add()
                        cp(cw[1 - b][:, :], conv[:, bass.ds(i * 2 + (n0 + b + 1), 1), :].rearrange("p o t -> p (o t)")).then_inc(taps_ready, 1)
                        lat, cx = padded(UP[b])
                        acc = ACC[b][:, CTX:TOK].rearrange("p (h w) -> p h w", w=GRID_W)
                        taps = [k for k in range(9) if k != 4]
                        dve.wait_ge(taps_ready, conv_n.now())
                        for j, k in enumerate(taps):
                            if tokens == TOK and j < 2:
                                o = 2 * j
                                mark(stt(ACC[b][:, 0:CTX], cx[:, o:o + CTX], cw[b][:, 3 + o:4 + o], ACC[b][:, 0:CTX], ALU.mult, ALU.add))
                            dy, dx = k // 3, k % 3
                            ins = stt(acc, lat[:, dy:dy + GRID_H, dx:dx + GRID_W], cw[b][:, k:k + 1], acc, ALU.mult, ALU.add)
                            if j < len(taps) - 1:
                                link(ins)
                            else:
                                ins.then_inc(conv_done, 1)
                        tile.add()
                        dve.wait_ge(gelu_done, conv_n.now())
                        dve.wait_ge(tile_done, tile.now())
                        tt(ACC[b][:, t0:TOK], ACC[b][:, t0:TOK], SLOT[1][:, PE0 - tokens:PE0], ALU.mult).then_inc(evacuated[1], 1)
                        if b == 1 and adds:
                            rows.add()
                            ada_add(col)
                        dve.wait_ge(g_hi, conv_n.now())
                        tt(GL[:, bass.ds(i * 2 + b, 1), t0:TOK].rearrange("p o t -> p (o t)"), ACC[b][:, t0:TOK],
                           GH[:, bass.ds(i * 2 + b, 1), t0:TOK].rearrange("p o t -> p (o t)").bitcast(F32), ALU.subtract).then_inc(g_lo, 1)

                group = 12
                for g, n in enumerate(GROUPS):
                    peel = int(layer == 0 and g == 0)
                    adds = int(layer == 0)
                    if peel:
                        body(0, False)
                    counts = [(tile, 4), (conv_n, 2), (steps, 2 * (7 + (2 if tokens == TOK else 0))), (rows, adds)]
                    loop(n // 2 - peel, counts, lambda i: body(i + peel, adds, i * 4 + 4 * group))
                    group += n // 2 - peel
                    n0 += n
                    (residual if g < len(GROUPS) - 1 else last_residual)(tokens, 48 * layer + G2 * KC)
                    if adds and g < 2:
                        rows.add()
                        ada_add(4 * group)
                        group += 1

            feed_forward(TOK, 0)
            norm_dve(TOK, norm_g[0][:, 1, :], 48 + SC1 * KC, 48 + SH1 * KC)

            ts(nsink[:, :], part("sink"), -1.0, None, ALU.mult).then_inc(roped, 1)
            nc.vector.memset(hold[:, :], 0.0).then_inc(roped, 1)
            dve.wait_ge(roped, 2)
            dve.wait_ge(rope_done, 48)
            rot, unit, pair, block_n = Tally(), Tally(), Tally(), Tally()

            def rope_one(dst, b):
                rot.add()
                dve.wait_ge(rot_done, rot.now())
                mark(tt(dst, RAW[b][:, :], rope[:, 0, :], ALU.mult))
                mark(tt(ROT[:, :], MA[:, 0:LAT], rope[:, 1, :], ALU.mult))
                settle()
                tt(dst, dst, ROT[:, :], ALU.add).then_inc(roped, 1)

            def softmax(u, i):
                if u < len(UNITS):
                    bi, half, r = UNITS[u]
                    hd = bass.ds(i * 8 + (half * 4 + r), 1)
                    n = 2 + window(bi)[1]
                    dve.wait_ge(at_scores, unit.times(1, (u + 1)))
                    mark(nc.vector.tensor_reduce(mx[u % 2][:, :], (MB, MA)[u % 2][:, PC0:PC0 + n * P], AX.X, ALU.max))
                w = u - 2
                if w >= 0:
                    dve.wait_ge(probs_ready, unit.times(1, (w + 1)))
                    mark(tt(den[w % 4][:, :], den[w % 4][:, :], es[w % 4][:, :], ALU.add))
                if u < len(UNITS):
                    dve.wait_ge(dve_step, steps.now(int(w >= 0)))
                    ts(nm[u % 2][:, :], mx[u % 2][:, :], -AT_SCALE, nsink[:, hd], ALU.mult, ALU.min).then_inc(row_max, 1)
                if w >= 0:
                    settle()
                    link(nc.vector.reciprocal(rden[w % 2][:, :], den[w % 4][:, :]))
                    n = 2 + window(UNITS[w][0])[1]
                    ts(PB[w % 3][:, 0:n * P], PB[w % 3][:, 0:n * P], rden[w % 2][:, :], None, ALU.mult).then_inc(probs_scaled, 1)

            def at_evac(bi, i):
                dve.wait_ge(pv_done, pair.now() + 2 * (bi + 1))
                cp(Y[:, bass.ds(i * 4, 4), CTX + bi * P:CTX + (bi + 1) * P], SLOT[1][:, 0:512].rearrange("p (r q) -> p r q", q=P)).then_inc(at_out, 1)

            def two_key_heads(i):
                rope_one(KT[:, CTX:TOK], 0)
                for r in range(4):
                    rope_one(QT[:, r, :], (r + 1) % 2)
                for u in range(len(UNITS) + 2):
                    softmax(u, i)
                    w = u - 4
                    if w % 8 == 0 and w > 0:
                        at_evac(w // 8 - 1, i)
                at_evac(3, i)
                unit.add(32)
                pair.add(8)
                tile.add(6)

            loop(2, [(tile, 6), (rot, 5), (unit, 32), (pair, 8), (steps, 10 + 3 * 32)], two_key_heads)
            mixer_lo(LAT)
            last_residual(LAT, 48 + G1 * KC)
            norm_dve(LAT, norm_g[1][:, 1, :], 48 + SC2 * KC, 48 + SH2 * KC)
            feed_forward(LAT, 1)
            norm_dve(LAT, fin_g, None, None)


def kernel(**inputs):
    import ml_dtypes
    import numpy as np
    import concourse.bacc as bacc
    from concourse.bass_utils import run_bass_kernel_spmd

    a = {k: np.asarray(v) for k, v in inputs.items()}
    f = np.float32

    def cols(v):
        return np.ascontiguousarray(v.reshape(-1, P).T)

    def tiles(w):
        k, n = w.shape
        if k < D:
            w = np.concatenate([w, np.zeros((D - k, n), w.dtype)])
        return w.reshape(KC, P, n // P, P).transpose(2, 1, 0, 3)

    x = np.concatenate([a["ctx"][0], a["x"][0]]).T.reshape(KC, P, TOK).transpose(1, 0, 2)

    wq = a["at_w_qkv"][0]
    nq = 1024
    heads = [(g * 4 + r) for kt in range(2) for r in range(4) for g in (2 * kt, 2 * kt + 1)]
    perm = np.concatenate([np.arange(h * 64, h * 64 + 64) for h in heads])
    at_cols = []
    for kt in range(2):
        at_cols += [np.arange(nq + kt * P, nq + (kt + 1) * P)]
        at_cols += [perm[(4 * kt + r) * P:(4 * kt + r + 1) * P] for r in range(4)]
        at_cols += [np.arange(nq + 256 + kt * P, nq + 256 + (kt + 1) * P)]
    at_cols = np.concatenate(at_cols)

    def feed(layer):
        up, down = a["ffn_w_up"][layer], a["ffn_w_down"][layer]
        u, v = tiles(up[:, :FF]), tiles(up[:, FF:])
        out, at = [], 0
        for n in GROUPS:
            for c in range(at, at + n):
                out += [u[c:c + 1], v[c:c + 1]]
            out.append(tiles(down[at * P:(at + n) * P]))
            at += n
        return out

    hg = tiles(a["hg_w_in"][0]).reshape(5, HEADS, P, KC, P)
    hg = hg[[3, 4, 0, 1, 2]].transpose(1, 0, 2, 3, 4).reshape(5 * HEADS, P, KC, P)
    w = np.concatenate([hg, tiles(a["hg_w_out"][0])] + feed(0) + [tiles(wq[:, at_cols]), tiles(a["at_w_out"][0][perm])] + feed(1))
    assert w.shape[0] == TILES, (w.shape, TILES)

    ada = a["ada_w"].reshape(2, 4, 2, P, 12, 512).transpose(0, 4, 1, 3, 2, 5).reshape(96, P, 1024)

    taps = np.concatenate([a["ffn_conv_w"].reshape(2, 9, FC, P), a["ffn_conv_b"].reshape(2, 1, FC, P)], axis=1)
    taps = taps.transpose(3, 0, 2, 1).reshape(P, 2 * FC * 10)
    cc = np.stack([a["c"][0], a["c_ctx"]], axis=1)
    order = [g * 4 + r for kt in range(2) for g in (2 * kt, 2 * kt + 1) for r in range(4)]
    packed = {
        "c": cc.reshape(KC, P, 2).transpose(1, 0, 2).reshape(P, 2 * KC),
        "ada_b": cols(a["ada_b"].reshape(-1)), "n1": cols(a["norm1_g"].reshape(-1)), "n2": cols(a["norm2_g"].reshape(-1)),
        "conv": np.concatenate([taps, np.zeros((P, 10), f)], axis=1),
        "lb": cols(a["hg_lb_logits"].reshape(-1)), "hgn": cols(a["hg_norm_g"].reshape(-1)),
        "bqkv": cols(a["at_b_qkv"][0][at_cols]), "sink": np.broadcast_to(a["at_sink"][0][order], (P, 16)),
        "fin": cols(a["final_norm_g"]),
    }
    small = np.concatenate([packed[n].astype(f, copy=False) for n in SMALL], axis=1)
    assert small.shape[1] == NSMALL

    i = np.arange(P)
    masks = np.zeros((P, LEVELS + 1, P), f)
    for n in range(LEVELS):
        masks[:, n] = ((i[:, None] >> (n + 1)) == (i[None] >> (n + 1))) & ((i[:, None] >> n) != (i[None] >> n))
    masks[:, LEVELS] = i[:, None] == i[None]
    t = np.arange(LAT)
    inv = (10000.0 ** (-np.arange(0, 32, 2, dtype=f) / 32)).astype(f)
    row, col = (t // GRID_W).astype(f), (t % GRID_W).astype(f)
    ang = np.concatenate([row[:, None] * inv] * 2 + [col[:, None] * inv] * 2, axis=1)
    rope = np.stack([np.tile(np.cos(ang).T, (2, 1)), np.tile(np.sin(ang).T, (2, 1))], axis=1).astype(f)
    rot = np.zeros((P, P), f)
    for m in range(P):
        rot[(m + 16, m) if m % 32 < 16 else (m - 16, m)] = -1.0 if m % 32 < 16 else 1.0
    tri = np.zeros((P, 3, P), np.float32)
    tri[:, 0] = np.where(i[None] >= i[:, None], 0.0, -1e30)
    tri[:, 1] = np.where(i[None] <= i[:, None], 0.0, -1e30)
    tri[:, 2] = np.eye(P)
    tri = tri.astype(ml_dtypes.bfloat16)

    arrays = {
        "small": small, "x": x, "ada": ada, "w": w, "ident": np.eye(P, dtype=f), "masks": masks.reshape(P, -1),
        "rope": rope, "rot": rot, "tri": tri,
    }
    arrays = {k: np.ascontiguousarray(v) for k, v in arrays.items()}
    nc = bacc.Bacc("TRN2", target_bir_lowering=False, num_devices=1)
    aps = [nc.dram_tensor(f"in_{n}", v.shape, mybir.dt.from_np(v.dtype), kind="ExternalInput").ap() for n, v in arrays.items()]
    out = nc.dram_tensor("out", (P, KC, LAT), F32, kind="ExternalOutput").ap()
    trunk(nc, *aps, out)
    r = run_bass_kernel_spmd(nc, [{f"in_{n}": v for n, v in arrays.items()}], core_ids=[0])
    y = r.results[0]["out"]
    return np.ascontiguousarray(y.transpose(2, 1, 0).reshape(1, LAT, D))
```
